# Optimizing a Trainium2 kernel written in Bass

```python
import math
import jax, jax.numpy as jnp
from jax import lax
import numpy as np

D_MODEL = 2048
BATCH = 1
SEQ = 256
DEPTH = 1

CHUNK = 64
N_MIXERS = 4
CONV_KERNEL = 31
LN_EPS = 1e-5
RWKV_HEAD_DIM = 64
RWKV_HEADS = D_MODEL // RWKV_HEAD_DIM
DECAY_LORA = 96
AAA_LORA = 96
GATE_LORA = 256
GN_EPS = 64e-5
SHORT_KERNEL = 3
FOX_HEAD_DIM = 128
FOX_HEADS = D_MODEL // FOX_HEAD_DIM
Q_BLOCK = 128
D_FF = 4 * D_MODEL
RMS_EPS = 1e-6


def _n_layers_of(m):
    return (DEPTH - m + N_MIXERS - 1) // N_MIXERS

def rmsnorm(x, g):
    xf = x.astype(jnp.float32)
    y = xf * lax.rsqrt(jnp.mean(xf * xf, axis=-1, keepdims=True) + RMS_EPS)
    return (y * g.astype(jnp.float32)).astype(x.dtype)

def layernorm(x, g, b):
    xf = x.astype(jnp.float32)
    mu = jnp.mean(xf, axis=-1, keepdims=True)
    var = jnp.mean(jnp.square(xf - mu), axis=-1, keepdims=True)
    y = (xf - mu) * lax.rsqrt(var + LN_EPS)
    return (y * g.astype(jnp.float32) + b.astype(jnp.float32)).astype(x.dtype)

def causal_dwconv(x, w):
    K = w.shape[0]
    return lax.conv_general_dilated(
        x, w[:, None, :].astype(x.dtype), window_strides=(1,), padding=[(K - 1, 0)],
        dimension_numbers=('NWC', 'WIO', 'NWC'), feature_group_count=x.shape[-1])

def conformer_conv(h, w_in, b_in, dw, dw_b, ln_g, ln_b, w_out, b_out):
    u = h @ w_in + b_in
    val, gate = jnp.split(u, 2, axis=-1)
    u = val * jax.nn.sigmoid(gate)
    u = causal_dwconv(u, dw) + dw_b
    u = jax.nn.silu(layernorm(u, ln_g, ln_b))
    return u @ w_out + b_out

def rwkv7_time_mix(h, mu, w_rkv, w0, w1, w2, a0, a1, a2, g1, g2, k_k, k_a, r_k, gn_g, gn_b, w_o):
    B, T, D = h.shape
    H, N = RWKV_HEADS, RWKV_HEAD_DIM
    f32 = jnp.float32
    xx = jnp.pad(h, ((0, 0), (1, 0), (0, 0)))[:, :T] - h
    xr, xw, xk, xv, xa, xg = (h + xx * mu[i] for i in range(6))
    r = xr @ w_rkv[0]
    k = xk @ w_rkv[1]
    v = xv @ w_rkv[2]
    w = -jax.nn.softplus(-(w0 + jnp.tanh(xw @ w1) @ w2).astype(f32)) - 0.5
    a = jax.nn.sigmoid(a0 + (xa @ a1) @ a2)
    g = jax.nn.sigmoid(xg @ g1) @ g2
    kk = (k * k_k).astype(f32).reshape(B, T, H, N)
    kk = kk / jnp.maximum(jnp.sqrt(jnp.sum(kk * kk, axis=-1, keepdims=True)), 1e-12)
    k = k * (1 + (a - 1) * k_a)

    def heads(t):
        return t.astype(f32).reshape(B, T, H, N)

    r_h, k_h, v_h, a_h = heads(r), heads(k), heads(v), heads(a)
    decay = jnp.exp(-jnp.exp(w)).reshape(B, T, H, N)

    def to_chunks(t):
        return t.transpose(1, 0, 2, 3).reshape(T // CHUNK, CHUNK, B, H, N)

    xs = tuple(to_chunks(t) for t in (r_h, decay, k_h, v_h, -kk, kk * a_h))

    def frame_step(S, inp):
        r_t, w_t, k_t, v_t, a_t, b_t = inp
        sa = jnp.einsum('bhij,bhj->bhi', S, a_t)
        S = S * w_t[:, :, None, :] + sa[..., None] * b_t[:, :, None, :] + v_t[..., None] * k_t[:, :, None, :]
        y = jnp.einsum('bhij,bhj->bhi', S, r_t)
        return S, y

    def chunk_step(S, chunk):
        return lax.scan(frame_step, S, chunk)

    S0 = jnp.zeros((B, H, N, N), f32)
    _, y = lax.scan(chunk_step, S0, xs)
    y = y.reshape(T, B, H, N).transpose(1, 0, 2, 3)
    mean = jnp.mean(y, axis=-1, keepdims=True)
    var = jnp.mean(jnp.square(y - mean), axis=-1, keepdims=True)
    y = ((y - mean) * lax.rsqrt(var + GN_EPS)).reshape(B, T, D) * gn_g.astype(f32) + gn_b.astype(f32)
    bonus = (jnp.sum(r_h * k_h * r_k.astype(f32), axis=-1, keepdims=True) * v_h).reshape(B, T, D)
    y = (y + bonus).astype(h.dtype)
    return (y * g) @ w_o

def short_conv(h, w_in, conv_w, w_out):
    u = h @ w_in
    gate_b, gate_c, hv = jnp.split(u, 3, axis=-1)
    z = causal_dwconv(gate_c * hv, conv_w)
    return (gate_b * z) @ w_out

def fox_attention(h, w_qkvf, b_f, w_o):
    B, T, D = h.shape
    H, Dh = FOX_HEADS, FOX_HEAD_DIM
    f32 = jnp.float32
    u = h @ w_qkvf

    def heads(t):
        return t.reshape(B, T, H, Dh).transpose(0, 2, 1, 3)

    q, k, v = heads(u[..., :D]), heads(u[..., D:2 * D]), heads(u[..., 2 * D:3 * D])
    log_f = jax.nn.log_sigmoid((u[..., 3 * D:] + b_f).astype(f32))
    c = jnp.cumsum(log_f, axis=1).transpose(0, 2, 1)
    scale = 1.0 / math.sqrt(Dh)
    outs = []
    for blk in range(T // Q_BLOCK):
        q0 = blk * Q_BLOCK
        q1 = q0 + Q_BLOCK
        s = jnp.einsum('bhqd,bhkd->bhqk', q[:, :, q0:q1], k[:, :, :q1]).astype(f32) * scale
        s = s + c[:, :, q0:q1, None] - c[:, :, None, :q1]
        mask = (q0 + jnp.arange(Q_BLOCK))[:, None] >= jnp.arange(q1)[None, :]
        s = jnp.where(mask, s, -jnp.inf)
        p = jax.nn.softmax(s, axis=-1).astype(v.dtype)
        outs.append(jnp.einsum('bhqk,bhkd->bhqd', p, v[:, :, :q1]))
    o = jnp.concatenate(outs, axis=2).transpose(0, 2, 1, 3).reshape(B, T, D)
    return o @ w_o

def sq_relu_mlp(h, w1, w2):
    return jnp.square(jax.nn.relu(h @ w1)) @ w2

def first_inputs(seed: int = 0) -> dict:
    key = jax.random.key(seed)
    ks = iter(jax.random.split(key, 48))
    D = D_MODEL
    nA, nB, nC, nD = (_n_layers_of(m) for m in range(N_MIXERS))
    H, N = RWKV_HEADS, RWKV_HEAD_DIM

    def nrm(shape, scale):
        return jax.random.normal(next(ks), shape, jnp.float32) * scale

    def gain(shape):
        return 1.0 + nrm(shape, 0.02)

    inp = {}
    inp["x"] = nrm((BATCH, SEQ, D), 1.0)
    inp["norm1_g"] = gain((DEPTH, D))
    inp["norm2_g"] = gain((DEPTH, D))
    inp["mlp_w1"] = nrm((DEPTH, D, D_FF), D ** -0.5)
    inp["mlp_w2"] = nrm((DEPTH, D_FF, D), D_FF ** -0.5)
    inp["cc_w_in"] = nrm((nA, D, 2 * D), D ** -0.5)
    inp["cc_b_in"] = nrm((nA, 2 * D), 0.02)
    inp["cc_dw"] = nrm((nA, CONV_KERNEL, D), CONV_KERNEL ** -0.5)
    inp["cc_dw_b"] = nrm((nA, D), 0.02)
    inp["cc_ln_g"] = gain((nA, D))
    inp["cc_ln_b"] = nrm((nA, D), 0.02)
    inp["cc_w_out"] = nrm((nA, D, D), D ** -0.5)
    inp["cc_b_out"] = nrm((nA, D), 0.02)
    inp["rw_mu"] = jax.random.uniform(next(ks), (nB, 6, D), jnp.float32)
    inp["rw_w_rkv"] = nrm((nB, 3, D, D), D ** -0.5)
    inp["rw_w0"] = jax.random.uniform(next(ks), (nB, D), jnp.float32, -6.0, -1.0)
    inp["rw_w1"] = nrm((nB, D, DECAY_LORA), D ** -0.5)
    inp["rw_w2"] = nrm((nB, DECAY_LORA, D), 0.5 * DECAY_LORA ** -0.5)
    inp["rw_a0"] = nrm((nB, D), 0.02)
    inp["rw_a1"] = nrm((nB, D, AAA_LORA), D ** -0.5)
    inp["rw_a2"] = nrm((nB, AAA_LORA, D), AAA_LORA ** -0.5)
    inp["rw_g1"] = nrm((nB, D, GATE_LORA), D ** -0.5)
    inp["rw_g2"] = nrm((nB, GATE_LORA, D), GATE_LORA ** -0.5)
    inp["rw_k_k"] = 0.85 + nrm((nB, D), 0.1)
    inp["rw_k_a"] = 1.0 + nrm((nB, D), 0.1)
    inp["rw_r_k"] = nrm((nB, H, N), 0.1)
    inp["rw_gn_g"] = gain((nB, D))
    inp["rw_gn_b"] = nrm((nB, D), 0.02)
    inp["rw_w_o"] = nrm((nB, D, D), D ** -0.5)
    inp["sc_w_in"] = nrm((nC, D, 3 * D), D ** -0.5)
    inp["sc_conv_w"] = nrm((nC, SHORT_KERNEL, D), SHORT_KERNEL ** -0.5)
    inp["sc_w_out"] = nrm((nC, D, D), D ** -0.5)
    w_qkv = nrm((nD, D, 3 * D), D ** -0.5)
    w_f = nrm((nD, D, FOX_HEADS), 0.1 * D ** -0.5)
    inp["fx_w_qkvf"] = jnp.concatenate([w_qkv, w_f], axis=-1)
    inp["fx_b_f"] = jax.random.uniform(next(ks), (nD, FOX_HEADS), jnp.float32, 1.0, 5.0)
    inp["fx_w_o"] = nrm((nD, D, D), D ** -0.5)
    inp["final_g"] = gain((D,))
    return inp

def first_block(x, norm1_g, norm2_g, mlp_w1, mlp_w2,
              cc_w_in, cc_b_in, cc_dw, cc_dw_b, cc_ln_g, cc_ln_b, cc_w_out, cc_b_out,
              rw_mu, rw_w_rkv, rw_w0, rw_w1, rw_w2, rw_a0, rw_a1, rw_a2, rw_g1, rw_g2,
              rw_k_k, rw_k_a, rw_r_k, rw_gn_g, rw_gn_b, rw_w_o,
              sc_w_in, sc_conv_w, sc_w_out,
              fx_w_qkvf, fx_b_f, fx_w_o, final_g):
    for i in range(DEPTH):
        m, j = i % N_MIXERS, i // N_MIXERS
        h = rmsnorm(x, norm1_g[i])
        if m == 0:
            y = conformer_conv(h, cc_w_in[j], cc_b_in[j], cc_dw[j], cc_dw_b[j],
                               cc_ln_g[j], cc_ln_b[j], cc_w_out[j], cc_b_out[j])
        elif m == 1:
            y = rwkv7_time_mix(h, rw_mu[j], rw_w_rkv[j], rw_w0[j], rw_w1[j], rw_w2[j],
                               rw_a0[j], rw_a1[j], rw_a2[j], rw_g1[j], rw_g2[j],
                               rw_k_k[j], rw_k_a[j], rw_r_k[j], rw_gn_g[j], rw_gn_b[j], rw_w_o[j])
        elif m == 2:
            y = short_conv(h, sc_w_in[j], sc_conv_w[j], sc_w_out[j])
        else:
            y = fox_attention(h, fx_w_qkvf[j], fx_b_f[j], fx_w_o[j])
        x = x + y
        x = x + sq_relu_mlp(rmsnorm(x, norm2_g[i]), mlp_w1[i], mlp_w2[i])
    return rmsnorm(x, final_g)


HEAD_DIM = 128
N_GDN_HEADS = 8
N_MOBA_HEADS = 8
GDN_WIDTH = N_GDN_HEADS * HEAD_DIM
MOBA_WIDTH = N_MOBA_HEADS * HEAD_DIM
MIX_WIDTH = GDN_WIDTH + MOBA_WIDTH
IN_PROJ_WIDTH = 4 * GDN_WIDTH + 2 * N_GDN_HEADS + 3 * MOBA_WIDTH
GDN_CONV = 4
GDN_CHUNK = 64
MOBA_BLOCK = 256
MOBA_TOPK = 3
MOBA_Q_CHUNK = 64
REL_BUCKETS = 32
REL_MAX_DIST = 128
MEM_LEN = 256
N_XATTN_HEADS = 4
XATTN_WIDTH = N_XATTN_HEADS * HEAD_DIM
D_FF_2 = 5632
FFN_CONV = 3
EPS = 1e-6
NEG = -1e30


def rmsnorm_2(x, g):
    xf = x.astype(jnp.float32)
    y = xf * lax.rsqrt(jnp.mean(xf * xf, axis=-1, keepdims=True) + EPS)
    return (y * g.astype(jnp.float32)).astype(x.dtype)

def l2norm(x):
    xf = x.astype(jnp.float32)
    return (xf * lax.rsqrt(jnp.sum(xf * xf, axis=-1, keepdims=True) + EPS)).astype(x.dtype)

def causal_dwconv_2(x, w):
    K = w.shape[0]
    S = x.shape[1]
    xp = jnp.pad(x, ((0, 0), (K - 1, 0), (0, 0)))
    return sum(xp[:, j:j + S] * w[j] for j in range(K))

def rel_bucket(rel):
    n = jnp.maximum(-rel, 0)
    max_exact = REL_BUCKETS // 2
    nf = jnp.maximum(n, 1).astype(jnp.float32)
    large = max_exact + (jnp.log(nf / max_exact) / math.log(REL_MAX_DIST / max_exact)
                         * (REL_BUCKETS - max_exact)).astype(jnp.int32)
    large = jnp.minimum(large, REL_BUCKETS - 1)
    return jnp.where(n < max_exact, n, large)

def gated_delta_rule(q, k, v, g, beta):
    out_dtype = v.dtype
    B, H, S, Dk = q.shape
    Dv = v.shape[-1]
    C = GDN_CHUNK
    N = S // C
    f32 = jnp.float32
    q = (q.astype(f32) * Dk ** -0.5).reshape(B, H, N, C, Dk)
    k = k.astype(f32).reshape(B, H, N, C, Dk)
    v = v.astype(f32).reshape(B, H, N, C, Dv)
    g = g.astype(f32).reshape(B, H, N, C)
    beta = beta.astype(f32).reshape(B, H, N, C)
    G = jnp.cumsum(g, axis=-1)
    tri_incl = jnp.tril(jnp.ones((C, C), dtype=bool))
    tri_strict = jnp.tril(jnp.ones((C, C), dtype=bool), -1)
    decay = jnp.exp(jnp.where(tri_incl, G[..., :, None] - G[..., None, :], NEG))
    kb = k * beta[..., None]
    A = jnp.where(tri_strict, jnp.einsum('bhnid,bhnjd->bhnij', kb, k) * decay, 0.0)
    eye = jnp.eye(C, dtype=f32)
    T = lax.linalg.triangular_solve(eye + A, jnp.broadcast_to(eye, A.shape),
                                    left_side=True, lower=True)
    u = jnp.einsum('bhnij,bhnjd->bhnid', T, v * beta[..., None])
    w = jnp.einsum('bhnij,bhnjd->bhnid', T, kb * jnp.exp(G)[..., None])
    qk = jnp.einsum('bhnid,bhnjd->bhnij', q, k) * decay
    q_dec = q * jnp.exp(G)[..., None]
    k_dec = k * jnp.exp(G[..., -1:] - G)[..., None]
    g_last = jnp.exp(G[..., -1])

    def step(state, xs):
        q_i, k_i, u_i, w_i, qk_i, gl_i = xs
        v_new = u_i - jnp.einsum('bhck,bhkv->bhcv', w_i, state)
        o_i = (jnp.einsum('bhck,bhkv->bhcv', q_i, state)
               + jnp.einsum('bhij,bhjv->bhiv', qk_i, v_new))
        state = state * gl_i[..., None, None] + jnp.einsum('bhck,bhcv->bhkv', k_i, v_new)
        return state, o_i

    xs = tuple(jnp.moveaxis(t, 2, 0) for t in (q_dec, k_dec, u, w, qk, g_last))
    state0 = jnp.zeros((B, H, Dk, Dv), f32)
    _, o = lax.scan(step, state0, xs)
    o = jnp.moveaxis(o, 0, 2).reshape(B, H, S, Dv)
    return o.astype(out_dtype)

def moba_attention(q, k, v, rel_bias):
    B, H, S, Dh = q.shape
    nb = -(-S // MOBA_BLOCK)
    s_pad = nb * MOBA_BLOCK
    pad = ((0, 0), (0, 0), (0, s_pad - S), (0, 0))
    k_blocks = jnp.pad(k, pad).reshape(B, H, nb, MOBA_BLOCK, Dh)
    v_blocks = jnp.pad(v, pad).reshape(B, H, nb, MOBA_BLOCK, Dh)
    k_mean = jnp.mean(k_blocks.astype(jnp.float32), axis=3).astype(k.dtype)
    n_sel = min(MOBA_TOPK, nb)
    scale = Dh ** -0.5
    n_chunks = S // MOBA_Q_CHUNK
    offs = jnp.arange(MOBA_BLOCK)
    rb_t = rel_bias.T
    head_idx = jnp.arange(H)[:, None, None, None]

    def per_batch(args):
        qb, kb, vb, kmb = args

        def per_chunk(c):
            q0 = c * MOBA_Q_CHUNK
            qc = lax.dynamic_slice_in_dim(qb, q0, MOBA_Q_CHUNK, axis=1)
            q_pos = q0 + jnp.arange(MOBA_Q_CHUNK)
            own = q0 // MOBA_BLOCK
            gate = jnp.einsum('hqd,hnd->hqn', qc, kmb).astype(jnp.float32)
            gate = jnp.where(jnp.arange(nb) < own, gate, NEG)
            _, idx = lax.top_k(gate, n_sel)
            valid = jnp.arange(n_sel) < own
            k_sel = jax.vmap(lambda blk, ix: blk[ix])(kb, idx)
            v_sel = jax.vmap(lambda blk, ix: blk[ix])(vb, idx)
            pos_sel = idx[..., None] * MOBA_BLOCK + offs
            bias_sel = rb_t[head_idx, rel_bucket(pos_sel - q_pos[None, :, None, None])]
            logit_sel = (jnp.einsum('hqd,hqnkd->hqnk', qc, k_sel).astype(jnp.float32) * scale
                         + bias_sel.astype(jnp.float32))
            logit_sel = jnp.where(valid[None, None, :, None], logit_sel, NEG)
            k_own = lax.dynamic_index_in_dim(kb, own, axis=1, keepdims=False)
            v_own = lax.dynamic_index_in_dim(vb, own, axis=1, keepdims=False)
            pos_own = own * MOBA_BLOCK + offs
            rel_own = pos_own[None, :] - q_pos[:, None]
            logit_own = (jnp.einsum('hqd,hkd->hqk', qc, k_own).astype(jnp.float32) * scale
                         + rb_t[:, rel_bucket(rel_own)].astype(jnp.float32))
            logit_own = jnp.where((rel_own <= 0)[None], logit_own, NEG)
            logits = jnp.concatenate(
                [logit_sel.reshape(H, MOBA_Q_CHUNK, n_sel * MOBA_BLOCK), logit_own], axis=-1)
            p = jax.nn.softmax(logits, axis=-1).astype(v.dtype)
            p_sel = p[..., :n_sel * MOBA_BLOCK].reshape(H, MOBA_Q_CHUNK, n_sel, MOBA_BLOCK)
            p_own = p[..., n_sel * MOBA_BLOCK:]
            return (jnp.einsum('hqnk,hqnkd->hqd', p_sel, v_sel)
                    + jnp.einsum('hqk,hkd->hqd', p_own, v_own))

        o = lax.map(per_chunk, jnp.arange(n_chunks))
        return o.transpose(1, 0, 2, 3).reshape(H, S, Dh)

    return lax.map(per_batch, (q, k_blocks, v_blocks, k_mean))

def to_heads(t, n_heads):
    B, S, _ = t.shape
    return t.reshape(B, S, n_heads, HEAD_DIM).transpose(0, 2, 1, 3)

def hybrid_mixer(x, norm_g, w_in, gdn_conv_w, a_log, dt_bias, gdn_norm_g,
                 moba_norm_g, rel_bias, w_out):
    B, S, _ = x.shape
    h = rmsnorm_2(x, norm_g)
    proj = h @ w_in
    i0 = 3 * GDN_WIDTH
    i1 = i0 + GDN_WIDTH
    i2 = i1 + N_GDN_HEADS
    i3 = i2 + N_GDN_HEADS
    qkv_a, z_a, b_a, a_a, qkv_b = (proj[..., :i0], proj[..., i0:i1], proj[..., i1:i2],
                                   proj[..., i2:i3], proj[..., i3:])
    qkv_a = jax.nn.silu(causal_dwconv_2(qkv_a, gdn_conv_w))
    q_a, k_a, v_a = [to_heads(t, N_GDN_HEADS) for t in jnp.split(qkv_a, 3, axis=-1)]
    beta = jax.nn.sigmoid(b_a).transpose(0, 2, 1)
    g = (-jnp.exp(a_log) * jax.nn.softplus(a_a + dt_bias)).transpose(0, 2, 1)
    o_a = gated_delta_rule(l2norm(q_a), l2norm(k_a), v_a, g, beta).transpose(0, 2, 1, 3)
    o_a = rmsnorm_2(o_a, gdn_norm_g) * jax.nn.silu(z_a.reshape(B, S, N_GDN_HEADS, HEAD_DIM))
    q_b, k_b, v_b = [to_heads(t, N_MOBA_HEADS) for t in jnp.split(qkv_b, 3, axis=-1)]
    o_b = moba_attention(q_b, k_b, v_b, rel_bias).transpose(0, 2, 1, 3)
    o_b = rmsnorm_2(o_b, moba_norm_g)
    o = jnp.concatenate([o_a.reshape(B, S, GDN_WIDTH), o_b.reshape(B, S, MOBA_WIDTH)], axis=-1)
    return o @ w_out

def cross_attention(x, mem, norm_g, mem_norm_g, w_xq, w_xkv, w_xo):
    B, S, _ = x.shape
    M = mem.shape[1]
    q = (rmsnorm_2(x, norm_g) @ w_xq).reshape(B, S, N_XATTN_HEADS, HEAD_DIM)
    kv = rmsnorm_2(mem, mem_norm_g) @ w_xkv
    k, v = [t.reshape(B, M, N_XATTN_HEADS, HEAD_DIM) for t in jnp.split(kv, 2, axis=-1)]
    logits = jnp.einsum('bshd,bmhd->bhsm', q, k).astype(jnp.float32) * HEAD_DIM ** -0.5
    p = jax.nn.softmax(logits, axis=-1).astype(v.dtype)
    o = jnp.einsum('bhsm,bmhd->bshd', p, v).reshape(B, S, XATTN_WIDTH)
    return o @ w_xo

def conv_ffn(x, norm_g, w_gate, w_up, conv_w, conv_b, w_down):
    h = rmsnorm_2(x, norm_g)
    gate = causal_dwconv_2(h @ w_gate, conv_w) + conv_b
    return (jax.nn.silu(gate) * (h @ w_up)) @ w_down

def second_inputs(seed: int = 0) -> dict:
    key = jax.random.key(seed)
    ks = jax.random.split(key, 24)
    f32 = jnp.float32
    L = DEPTH

    def nrm(k, shape, scale):
        return jax.random.normal(k, shape, f32) * scale

    def gain(k, shape):
        return 1.0 + 0.02 * jax.random.normal(k, shape, f32)

    dt = jnp.exp(jax.random.uniform(ks[6], (L, N_GDN_HEADS), f32, math.log(1e-3), math.log(1e-1)))
    return {
        "x": nrm(ks[0], (BATCH, SEQ, D_MODEL), 1.0),
        "mem": nrm(ks[1], (BATCH, MEM_LEN, D_MODEL), 1.0),
        "mix_norm_g": gain(ks[2], (L, D_MODEL)),
        "w_in": nrm(ks[3], (L, D_MODEL, IN_PROJ_WIDTH), D_MODEL ** -0.5),
        "gdn_conv_w": nrm(ks[4], (L, GDN_CONV, 3 * GDN_WIDTH), GDN_CONV ** -0.5),
        "gdn_a_log": jnp.log(jax.random.uniform(ks[5], (L, N_GDN_HEADS), f32, 1.0, 16.0)),
        "gdn_dt_bias": dt + jnp.log(-jnp.expm1(-dt)),
        "gdn_norm_g": gain(ks[7], (L, HEAD_DIM)),
        "moba_norm_g": gain(ks[8], (L, HEAD_DIM)),
        "rel_bias": nrm(ks[9], (REL_BUCKETS, N_MOBA_HEADS), 0.5),
        "w_out": nrm(ks[10], (L, MIX_WIDTH, D_MODEL), MIX_WIDTH ** -0.5),
        "xattn_norm_g": gain(ks[11], (L, D_MODEL)),
        "mem_norm_g": gain(ks[12], (L, D_MODEL)),
        "w_xq": nrm(ks[13], (L, D_MODEL, XATTN_WIDTH), D_MODEL ** -0.5),
        "w_xkv": nrm(ks[14], (L, D_MODEL, 2 * XATTN_WIDTH), D_MODEL ** -0.5),
        "w_xo": nrm(ks[15], (L, XATTN_WIDTH, D_MODEL), XATTN_WIDTH ** -0.5),
        "ffn_norm_g": gain(ks[16], (L, D_MODEL)),
        "w_gate": nrm(ks[17], (L, D_MODEL, D_FF_2), D_MODEL ** -0.5),
        "w_up": nrm(ks[18], (L, D_MODEL, D_FF_2), D_MODEL ** -0.5),
        "ffn_conv_w": nrm(ks[19], (L, FFN_CONV, D_FF_2), FFN_CONV ** -0.5),
        "ffn_conv_b": nrm(ks[20], (L, D_FF_2), 0.02),
        "w_down": nrm(ks[21], (L, D_FF_2, D_MODEL), D_FF_2 ** -0.5),
        "final_norm_g": gain(ks[22], (D_MODEL,)),
    }

def second_block(x, mem, mix_norm_g, w_in, gdn_conv_w, gdn_a_log, gdn_dt_bias, gdn_norm_g,
              moba_norm_g, rel_bias, w_out, xattn_norm_g, mem_norm_g, w_xq, w_xkv, w_xo,
              ffn_norm_g, w_gate, w_up, ffn_conv_w, ffn_conv_b, w_down, final_norm_g):
    for l in range(DEPTH):
        x = x + hybrid_mixer(x, mix_norm_g[l], w_in[l], gdn_conv_w[l], gdn_a_log[l],
                             gdn_dt_bias[l], gdn_norm_g[l], moba_norm_g[l], rel_bias, w_out[l])
        x = x + cross_attention(x, mem, xattn_norm_g[l], mem_norm_g[l], w_xq[l], w_xkv[l], w_xo[l])
        x = x + conv_ffn(x, ffn_norm_g[l], w_gate[l], w_up[l], ffn_conv_w[l], ffn_conv_b[l], w_down[l])
    return rmsnorm_2(x, final_norm_g)


def setup_inputs(seed=0):
    out = dict(first_inputs(seed))
    for name, value in second_inputs(seed + 1).items():
        if name != "x":
            out[name + "_2"] = value
    return out


def reference(
    x, norm1_g, norm2_g, mlp_w1, mlp_w2, cc_w_in, cc_b_in, cc_dw, cc_dw_b, cc_ln_g, cc_ln_b,
    cc_w_out, cc_b_out, rw_mu, rw_w_rkv, rw_w0, rw_w1, rw_w2, rw_a0, rw_a1, rw_a2, rw_g1, rw_g2,
    rw_k_k, rw_k_a, rw_r_k, rw_gn_g, rw_gn_b, rw_w_o, sc_w_in, sc_conv_w, sc_w_out, fx_w_qkvf,
    fx_b_f, fx_w_o, final_g, mem_2, mix_norm_g_2, w_in_2, gdn_conv_w_2, gdn_a_log_2,
    gdn_dt_bias_2, gdn_norm_g_2, moba_norm_g_2, rel_bias_2, w_out_2, xattn_norm_g_2,
    mem_norm_g_2, w_xq_2, w_xkv_2, w_xo_2, ffn_norm_g_2, w_gate_2, w_up_2, ffn_conv_w_2,
    ffn_conv_b_2, w_down_2, final_norm_g_2,
):
    x = first_block(
        x, norm1_g, norm2_g, mlp_w1, mlp_w2, cc_w_in, cc_b_in, cc_dw, cc_dw_b, cc_ln_g, cc_ln_b,
        cc_w_out, cc_b_out, rw_mu, rw_w_rkv, rw_w0, rw_w1, rw_w2, rw_a0, rw_a1, rw_a2, rw_g1,
        rw_g2, rw_k_k, rw_k_a, rw_r_k, rw_gn_g, rw_gn_b, rw_w_o, sc_w_in, sc_conv_w, sc_w_out,
        fx_w_qkvf, fx_b_f, fx_w_o, final_g,
    )
    return second_block(
        x, mem_2, mix_norm_g_2, w_in_2, gdn_conv_w_2, gdn_a_log_2, gdn_dt_bias_2, gdn_norm_g_2,
        moba_norm_g_2, rel_bias_2, w_out_2, xattn_norm_g_2, mem_norm_g_2, w_xq_2, w_xkv_2,
        w_xo_2, ffn_norm_g_2, w_gate_2, w_up_2, ffn_conv_w_2, ffn_conv_b_2, w_down_2,
        final_norm_g_2,
    )


_drawn_inputs = setup_inputs


def setup_inputs(seed=0):
    import zlib

    import numpy as np

    out = dict(_drawn_inputs(seed))
    spreads = {}
    factors = {'norm1_g': 3.925,
     'norm2_g': 2.963,
     'cc_b_in': 3.185,
     'cc_ln_g': 3.297,
     'cc_ln_b': 3.362,
     'mix_norm_g_2': 3.254,
     'gdn_norm_g_2': 8.0,
     'moba_norm_g_2': 4.376,
     'xattn_norm_g_2': 8.0,
     'mem_norm_g_2': 8.0,
     'ffn_norm_g_2': 12.363,
     'ffn_conv_b_2': 18.167,
     'final_norm_g_2': 7.895}
    for name, (base, spread) in spreads.items():
        noise = np.random.default_rng([zlib.crc32(name.encode()), seed]).standard_normal(out[name].shape)
        drawn = base * np.exp(spread * noise) if base else spread * noise
        out[name] = __import__('jax').numpy.asarray(drawn.astype(out[name].dtype))
    for name, factor in factors.items():
        out[name] = (out[name] * factor).astype(out[name].dtype)
    return out
```

```python
from contextlib import ExitStack

import numpy as np

import concourse.bass as bass
from concourse import mybir

F32 = mybir.dt.float32
F32R = mybir.dt.float32r
ALU = mybir.AluOpType
ACT = mybir.ActivationFunctionType
AX = mybir.AxisListType

P = 128
T = 256
TT = T // P
D = 2048
KT = D // P
COLS = 512
CT = COLS // P
SLOT_K = 2
DFF = 8192
MLP_CHUNK = 1024
DFF2 = 5632
CONV_K = 31
GDN_K = 4
FFN_K = 3
HD = 128
NG = 8
NM = 8
NX = 4
CHUNK = 64
GW = NG * HD
NEG = -1e30
RAW = 4
SPLIT = 4
BUCKETS = 32



class Engine:

    def __init__(self, queue, sem):
        self.q, self.sem, self.count, self.waited = queue, sem, 0, {}

    def mark(self, instruction):
        self.count += 1
        instruction.then_inc(self.sem, 1)
        return (self.sem, self.count)

    def now(self):
        return (self.sem, self.count)

    def after(self, *marks):
        need = {}

        def gather(m):
            if m is None:
                return
            if isinstance(m, list):
                for x in m:
                    gather(x)
                return
            sem, value = m
            if value > self.waited.get(sem.name, 0) and value > need.get(sem.name, (None, 0))[1]:
                need[sem.name] = (sem, value)

        gather(list(marks))
        for name, (sem, value) in need.items():
            self.q.wait_ge(sem, value)
            self.waited[name] = value


class Ring:

    def __init__(self, buffers):
        self.buffers, self.free, self.at = buffers, [None] * len(buffers), -1
        self.held = [False] * len(buffers)

    def take(self):
        for n in range(1, len(self.buffers) + 1):
            i = (self.at + n) % len(self.buffers)
            if not self.held[i]:
                self.at, self.held[i] = i, True
                return i, self.buffers[i], self.free[i]
        raise AssertionError("every buffer of the ring is held")

    def give(self, i, *marks):
        self.free[i], self.held[i] = list(marks), False


def step(engine, waits, instruction):
    engine.after(*waits)
    return engine.mark(instruction(engine.q))


class Operand:

    def __init__(self, hi, lo):
        self.hi, self.lo = hi, lo
        self.ready = [None] * hi.shape[1]
        self.read = None



def rel_buckets(distance):
    max_exact = BUCKETS // 2
    nf = np.maximum(distance, 1).astype(np.float32)
    large = max_exact + (np.log(nf / np.float32(max_exact)) / np.float32(np.log(128 / max_exact))
                         * np.float32(BUCKETS - max_exact)).astype(np.int32)
    return np.where(distance < max_exact, distance, np.minimum(large, BUCKETS - 1))


MASKS = ["identity", "ones", "cumsum", "same_chunk", "causal_neg", "merge1"] + [f"merge{n}_t" for n in range(1, 7)]
BIAS_W = 384


def masks():
    i, j = np.arange(P)[:, None], np.arange(P)[None, :]
    same = (i // CHUNK) == (j // CHUNK)
    out = {
        "identity": i == j,
        "ones": np.ones((P, P), bool),
        "cumsum": same & (i <= j),
        "same_chunk": same,
    }
    out = {k: v.astype(np.float32) for k, v in out.items()}
    out["causal_neg"] = np.where(same & (i >= j), 0, NEG).astype(np.float32)
    for n in range(1, 7):
        m = ((i >> n) == (j >> n)) & (((i >> (n - 1)) & 1) == 1) & (((j >> (n - 1)) & 1) == 0)
        if n == 1:
            out["merge1"] = m.astype(np.float32)
        out[f"merge{n}_t"] = m.T.astype(np.float32)
    return np.stack([out[k] for k in MASKS], axis=1)


def bucket_rows():
    distance = 255 - np.arange(BIAS_W)
    hot = (rel_buckets(np.maximum(distance, 0))[None, :] == np.arange(BUCKETS)[:, None]).astype(np.float32)
    neg = np.where(distance >= 0, 0, NEG).astype(np.float32)
    return hot, np.broadcast_to(neg, (NM, BIAS_W)).copy()


VECTORS = [("norm1_g", 16), ("norm2_g", 16), ("cc_b_in", 32), ("cc_dw_b", 16), ("cc_ln_g", 16),
           ("cc_ln_b", 16), ("cc_b_out", 16), ("final_g", 16), ("mix_norm_g_2", 16), ("gdn_norm_g_2", 1),
           ("moba_norm_g_2", 1), ("xattn_norm_g_2", 16), ("mem_norm_g_2", 16), ("ffn_norm_g_2", 16),
           ("ffn_conv_b_2", 44), ("final_norm_g_2", 16)]
FILTERS = [("cc_dw", 16, CONV_K), ("gdn_conv_w_2", 24, GDN_K), ("ffn_conv_w_2", 44, FFN_K)]


def columns():
    at, n = {}, 0
    for name, tiles in VECTORS:
        at[name] = n
        n += tiles
    for name, tiles, taps in FILTERS:
        at[name] = n
        n += tiles * taps
    return at, n


COL, N_COLS = columns()



class Program:
    def __init__(self, nc, stack, dram):
        self.nc, self.stack, self.dram = nc, stack, dram
        self.pe = Engine(nc.tensor, self.sem("pe_done"))
        self.dve = Engine(nc.vector, self.sem("dve_done"))
        self.act = Engine(nc.scalar, self.sem("act_done"))
        self.pool = Engine(nc.gpsimd, self.sem("pool_done"))
        self.sp = Engine(nc.sync, self.sem("sp_done"))
        self.dma_sems = {}
        self.lo_turn = 0

        self.x = self.sbuf("x_residual", [P, KT, T])
        self.x_ready = [None] * CT
        self.x_read = [None] * CT
        self.h = Operand(self.sbuf("h_hi", [P, KT, T], F32R), self.sbuf("h_lo", [P, KT, T], F32R))
        self.mem_k = self.sbuf("mem_k", [P, NX, T])
        self.mem_v = self.sbuf("mem_v", [P, TT, NX * HD])
        self.w_raw = [self.sbuf(f"w_raw{i}", [P, SLOT_K, COLS]) for i in range(RAW)]
        self.w_hi = [self.sbuf(f"w_hi{i}", [P, SLOT_K, COLS], F32R) for i in range(SPLIT)]
        self.w_lo = [self.sbuf(f"w_lo{i}", [P, SLOT_K, COLS], F32R) for i in range(SPLIT)]
        self.scratch = Ring([self.sbuf(f"scratch{i}", [P, CT, T]) for i in range(3)])
        self.sum_sq = self.sbuf("sum_sq", [P, 2, T])
        self.stat = self.sbuf("stat", [P, 2, T])
        self.sum_read = None
        self.stat_read = None
        self.mask = self.sbuf("masks", [P, len(MASKS), P])
        self.cols = self.sbuf("feature_columns", [P, N_COLS])
        self.eps = self.sbuf("epsilons", [P, 3])
        self.acc = Ring([self.psum(f"product{i}", [P, 2 * 512]) for i in range(2)])
        self.bank = Ring([self.psum(f"small{i}", [P, 512]) for i in range(4)])

    def sbuf(self, name, shape, dt=F32, stack=None):
        return (stack or self.stack).enter_context(self.nc.sbuf_tensor(name, shape, dt))[:]

    def psum(self, name, shape):
        return self.stack.enter_context(self.nc.psum_tensor(name, shape, F32))[:]

    def sem(self, name):
        return self.stack.enter_context(self.nc.semaphore(name))

    def col(self, name, i, n=1):
        return self.cols[:, COL[name] + i:COL[name] + i + n]

    def m(self, name):
        return self.mask[:, MASKS.index(name), :]

    def dma(self, engine, out, in_, name):
        if name not in self.dma_sems:
            self.dma_sems[name] = [self.sem(name), 0]
        s = self.dma_sems[name]
        s[1] += 16
        engine.q.dma_start(out, in_).then_inc(s[0], 16)
        return (s[0], s[1])

    def phase(self):
        engines = [self.pe, self.dve, self.act, self.pool]
        for e in engines:
            e.after(*[o.now() for o in engines])

    def plan_weights(self):
        d, plan = self.dram, []

        def block(name, col, k0=0, k=D):
            for r in range(k0, k0 + k, SLOT_K * P):
                w = d[name][r:r + SLOT_K * P, col:col + COLS]
                plan.append(((name, r, col), w.rearrange("(k p) n -> p k n", p=P)))

        for b in range(CT):
            block("cc_w_in", D + b * COLS)
            block("cc_w_in", b * COLS)
        for b in range(2):
            block("w_xkv_2", b * COLS)
        for b in range(CT):
            block("cc_w_out", b * COLS)
        for kind, c in mlp_order():
            if kind == "up":
                for b in range(MLP_CHUNK // COLS):
                    block("mlp_w1", c * MLP_CHUNK + b * COLS)
            else:
                for b in range(CT):
                    block("mlp_w2", b * COLS, c * MLP_CHUNK, MLP_CHUNK)
        for g in range(2):
            for part in range(4):
                block("w_in_2", part * GW + g * COLS)
        for b in range(6):
            block("w_in_2", 4 * GW + 2 * NG + b * COLS)
        for b in range(CT):
            block("w_out_2", b * COLS)
        block("w_xq_2", 0)
        for b in range(CT):
            block("w_xo_2", b * COLS, 0, NX * HD)
        for kind, c in ffn_order():
            if kind == "up":
                block("w_gate_2", c * COLS)
                block("w_up_2", c * COLS)
            else:
                for b in range(CT):
                    block("w_down_2", b * COLS, c * COLS, COLS)
        self.plan = plan
        n = len(plan)
        self.n_loaded = self.n_split = self.n_used = 0
        self.slot_landed = [None] * n
        self.slot_raw_read = [None] * n
        self.slot_split = [None] * n
        self.slot_used = [None] * n

    def load_slot(self):
        i = self.n_loaded
        if i >= len(self.plan):
            return
        self.n_loaded += 1
        if i >= RAW:
            self.sp.after(self.slot_raw_read[i - RAW])
        self.slot_landed[i] = self.dma(self.sp, self.w_raw[i % RAW], self.plan[i][1], f"w_landed{i % RAW}")

    def split_slot(self):
        i = self.n_split
        if i >= len(self.plan):
            return
        self.n_split += 1
        raw, hi, lo = self.w_raw[i % RAW], self.w_hi[i % SPLIT], self.w_lo[i % SPLIT]
        used = self.slot_used[i - SPLIT] if i >= SPLIT else None
        self.act.after(self.slot_landed[i], used)
        hi_done = self.act.mark(self.act.q.activation(hi, raw, ACT.Copy))
        e = self.pool if self.on_pool(i) else self.dve
        e.after(hi_done)
        lo_done = e.mark(e.q.tensor_tensor(lo, raw, hi.bitcast(F32), ALU.subtract))
        self.slot_raw_read[i] = [hi_done, lo_done]
        self.slot_split[i] = [hi_done, lo_done]
        self.load_slot()

    def on_pool(self, i):
        return self.pool_every and i % self.pool_every == 0

    def use_slot(self, name, row, col):
        i = self.n_used
        assert self.plan[i][0] == (name, row, col), (self.plan[i][0], (name, row, col))
        self.n_used += 1
        self.pe.after(self.slot_split[i])
        return i, self.w_hi[i % SPLIT], self.w_lo[i % SPLIT]

    def slot_done(self, i, mark):
        self.slot_used[i] = mark
        self.split_slot()

    def product(self, name, col, x, evict, row=0, k=None, tokens_out=False):
        k = x.hi.shape[1] if k is None else k
        slot, psum, free = self.acc.take()
        self.pe.after(free)
        q = self.pe.q
        for s in range(k // SLOT_K):
            i, hi, lo = self.use_slot(name, row + s * SLOT_K * P, col)
            last = None
            parts = range(TT) if tokens_out else range(CT)
            for part in parts:
                for kk in range(SLOT_K):
                    kt = s * SLOT_K + kk
                    self.pe.after(x.ready[kt])
                    if tokens_out:
                        out = psum[:, part * COLS:(part + 1) * COLS]
                        t = slice(part * P, (part + 1) * P)
                        triples = [(x.hi[:, kt, t], hi[:, kk, :]), (x.lo[:, kt, t], hi[:, kk, :]),
                                   (x.hi[:, kt, t], lo[:, kk, :])]
                        opens = True
                    else:
                        out = psum[:, part * T:(part + 1) * T]
                        n = slice(part * P, (part + 1) * P)
                        triples = [(hi[:, kk, n], x.hi[:, kt, :]), (hi[:, kk, n], x.lo[:, kt, :]),
                                   (lo[:, kk, n], x.hi[:, kt, :])]
                        opens = part % 2 == 0
                    for j, (stationary, moving) in enumerate(triples):
                        first, final = kt == 0 and j == 0, kt == k - 1 and j == 2
                        last = q.matmul(out, stationary, moving, start=first and opens, stop=final,
                                        skip_group_check=True)
            mark = self.pe.mark(last)
            x.read = mark
            if s == k // SLOT_K - 1:
                self.acc.give(slot, evict(psum, mark))
            self.slot_done(i, mark)
            yield

    def split_into(self, src, src_mark, x, first, n):
        hi, lo = x.hi[:, first:first + n, :], x.lo[:, first:first + n, :]
        self.act.after(src_mark, x.read)
        hi_done = self.act.mark(self.act.q.activation(hi, src, ACT.Copy))
        self.dve.after(hi_done)
        lo_done = self.dve.mark(self.dve.q.tensor_tensor(lo, src, hi.bitcast(F32), ALU.subtract))
        for i in range(first, first + n):
            x.ready[i] = [hi_done, lo_done]
        return [hi_done, lo_done]

    def add_squares(self, src, src_mark, g, which=0, square=True):
        act, dve = self.act, self.dve
        if square:
            i, sq, free = self.scratch.take()
            act.after(src_mark, free)
            done = act.mark(act.q.activation(sq, src, ACT.Square))
            read = [done]
        else:
            sq, done, read = src, src_mark, []
        out = self.sum_sq[:, which, :]
        tiles = sq.rearrange("p k t -> p t k")
        if g == 0:
            dve.after(done, self.sum_read)
            r = dve.mark(dve.q.tensor_reduce(out, tiles, AX.X, ALU.add))
            if square:
                self.scratch.give(i, r)
            read.append(r)
            self.sum_done = r
            return read
        part = self.partial
        dve.after(done, self.partial_read)
        r = dve.mark(dve.q.tensor_reduce(part, tiles, AX.X, ALU.add))
        if square:
            self.scratch.give(i, r)
        read.append(r)
        dve.after(r)
        self.sum_done = dve.mark(dve.q.tensor_tensor(out, out, part, ALU.add))
        self.partial_read = self.sum_done
        return read

    def total(self, which=0):
        i, bank, free = self.bank.take()
        self.pe.after(self.sum_done, free)
        out = bank[:, 0:T]
        done = self.pe.mark(self.pe.q.matmul(out, self.m("ones"), self.sum_sq[:, which, :], start=True, stop=True))
        self.sum_read = done
        return i, out, done

    def inverse_root(self, psum, mark, out, scale, eps, out_free=None):
        self.act.after(mark, out_free)
        root = self.act.mark(self.act.q.activation(out, psum, ACT.Sqrt, bias=self.eps[:, eps:eps + 1], scale=scale))
        self.dve.after(root)
        return root, self.dve.mark(self.dve.q.reciprocal(out, out))

    def rms_scale(self):
        i, psum, done = self.total()
        root, ready = self.inverse_root(psum, done, self.stat[:, 1, :], 1.0 / D, 0, self.stat_read)
        self.bank.give(i, root)
        return ready

    def norm_group(self, src, marks, gain, g, rstd_mark, out, out_free):
        self.dve.after(marks, rstd_mark, out_free)
        for t in range(CT):
            done = self.dve.mark(self.dve.q.scalar_tensor_tensor(
                out=out[:, t, :], in0=src[:, t, :], scalar=self.col(gain, g * CT + t),
                in1=self.stat[:, 1, :], op0=ALU.mult, op1=ALU.mult))
        return done

    def norm_to_operand(self, src, src_ready, gain, x):
        ready = self.rms_scale()
        readers = []
        for g in range(CT):
            i, tmp, free = self.scratch.take()
            done = self.norm_group(src[:, g * CT:(g + 1) * CT, :], src_ready[g], gain, g, ready, tmp, free)
            self.scratch.give(i, self.split_into(tmp, done, x, g * CT, CT))
            readers.append(done)
        self.stat_read = done
        return readers

    def norm_x(self, gain):
        for g, r in enumerate(self.norm_to_operand(self.x, self.x_ready, gain, self.h)):
            self.x_read[g] = [self.x_read[g], r]

    def residual(self, b, bias=None, sum_squares=True):
        def evict(psum, mark):
            x = self.x[:, b * CT:(b + 1) * CT, :]
            self.dve.after(mark, self.x_ready[b], self.x_read[b])
            y = psum.rearrange("p (k t) -> p k t", t=T)
            if bias is None:
                done = self.dve.mark(self.dve.q.tensor_tensor(x, x, y, ALU.add))
            else:
                for t in range(CT):
                    done = self.dve.mark(self.dve.q.scalar_tensor_tensor(
                        out=x[:, t, :], in0=y[:, t, :], scalar=self.col(bias, b * CT + t), in1=x[:, t, :],
                        op0=ALU.add, op1=ALU.add))
            self.x_ready[b], self.x_read[b] = done, None
            if sum_squares:
                self.x_read[b] = self.add_squares(x, done, b)
            return done
        return evict

    def constants(self):
        d = self.dram
        self.pe.after(self.dma(self.act, self.mask, d["masks"], "masks_landed"))
        landed = self.dma(self.act, self.cols, d["feature_columns"], "columns_landed")
        self.dve.after(landed, (self.dma_sems["masks_landed"][0], 16))
        self.act.after(landed, (self.dma_sems["masks_landed"][0], 16))
        self.pool.after(landed, (self.dma_sems["masks_landed"][0], 16))
        self.partial = self.sbuf("partial_sum", [P, T])
        self.partial_read = None
        for i, v in enumerate([1e-6, 1e-5, 128e-6]):
            done = self.pool.mark(self.pool.q.memset(self.eps[:, i:i + 1], v))
        self.act.after(done)


def mlp_order():
    n = DFF // MLP_CHUNK
    out = [("up", 0)]
    for c in range(1, n):
        out += [("up", c), ("down", c - 1)]
    return out + [("down", n - 1)]


def ffn_order():
    n = DFF2 // COLS
    out = [("up", 0)]
    for c in range(1, n):
        out += [("up", c), ("down", c - 1)]
    return out + [("down", n - 1)]


def run(*steps):
    for s in steps:
        for _ in s:
            pass



def conformer(p):
    d, dve, act, pool = p.dram, p.dve, p.act, p.pool
    stack = p.phase_stack
    mem = Operand(p.sbuf("mem_hi", [P, KT, T], F32R, stack), p.sbuf("mem_lo", [P, KT, T], F32R, stack))
    p.mid = mem
    u = p.sbuf("conv_out", [P, KT, T], stack=stack)
    mem_x = u
    gate = Ring([p.sbuf(f"gate{i}", [P, CT, T], stack=stack) for i in range(2)])
    glu = Ring([p.sbuf(f"glu{i}", [P, CT, CONV_K - 1 + T], stack=stack) for i in range(2)])

    for g in range(CT):
        tiles = slice(g * CT, (g + 1) * CT)
        p.x_ready[g] = p.dma(p.sp, p.x[:, tiles, :], d["x"][tiles].rearrange("k p t -> p k t"), f"x_landed{g}")
    for _ in range(RAW):
        p.load_slot()
    mem_ready = []
    for g in range(CT):
        tiles = slice(g * CT, (g + 1) * CT)
        mem_ready.append(p.dma(p.act, mem_x[:, tiles, :], d["mem"][tiles].rearrange("k p t -> p k t"), f"mem_landed{g}"))
    for i in range(2):
        glu.give(i, pool.mark(pool.q.memset(glu.buffers[i][:, :, 0:CONV_K - 1], 0.0)))

    for g in range(CT):
        tiles = slice(g * CT, (g + 1) * CT)
        p.x_read[g] = p.add_squares(p.x[:, tiles, :], p.x_ready[g], g)
    p.norm_x("norm1_g")
    for _ in range(SPLIT):
        p.split_slot()
    for g in range(CT):
        p.add_squares(mem_x[:, g * CT:(g + 1) * CT, :], mem_ready[g], g)
    u_free = p.norm_to_operand(mem_x, mem_ready, "mem_norm_g_2", mem)

    u_ready = [None] * CT
    gates = {}

    def evict_gate(b):
        def evict(psum, mark):
            i, out, free = gate.take()
            act.after(mark, free)
            for t in range(CT):
                done = act.mark(act.q.activation(out[:, t, :], psum[:, t * T:(t + 1) * T], ACT.Sigmoid,
                                                 bias=p.col("cc_b_in", KT + b * CT + t)))
            gates[b] = (i, out, done)
            return done
        return evict

    def evict_value(b):
        def evict(psum, mark):
            gi, g, g_done = gates[b]
            i, out, free = glu.take()
            dve.after(mark, g_done, free)
            for t in range(CT):
                done = dve.mark(dve.q.scalar_tensor_tensor(
                    out=out[:, t, CONV_K - 1:], in0=psum[:, t * T:(t + 1) * T],
                    scalar=p.col("cc_b_in", b * CT + t), in1=g[:, t, :], op0=ALU.add, op1=ALU.mult))
            gate.give(gi, done)
            todo.append((b, i, out, done))
            return done
        return evict

    todo = []

    def convolve(b, i, src, mark):
        dve.after(mark, u_free[b])
        done = [None] * CT
        for j in range(CONV_K):
            for t in range(CT):
                out, tap = u[:, b * CT + t, :], src[:, t, j:j + T]
                w = p.col("cc_dw", (b * CT + t) * CONV_K + j)
                dve.after(done[t])
                if j == 0:
                    ins = dve.q.tensor_scalar(out, tap, w, p.col("cc_dw_b", b * CT + t), ALU.mult, ALU.add)
                else:
                    ins = dve.q.scalar_tensor_tensor(out=out, in0=tap, scalar=w, in1=out, op0=ALU.mult, op1=ALU.add)
                done[t] = dve.mark(ins)
            if j % 2 == 1:
                yield
        glu.give(i, done[-1])
        u_ready[b] = done[-1]
        p.add_squares(u[:, b * CT:(b + 1) * CT, :], done[-1], b, which=1, square=False)

    def keys(psum, mark):
        act.after(mark)
        done = act.mark(act.q.activation(p.mem_k, psum.rearrange("p (k t) -> p k t", t=T), ACT.Copy))
        p.mem_k_ready = done
        return done

    def values(psum, mark):
        act.after(mark)
        done = act.mark(act.q.activation(p.mem_v, psum.rearrange("p (k n) -> p k n", n=COLS), ACT.Copy))
        p.mem_v_ready = done
        return done

    def products():
        for b in range(CT):
            yield from p.product("cc_w_in", D + b * COLS, p.h, evict_gate(b))
            yield from p.product("cc_w_in", b * COLS, p.h, evict_value(b))
        yield from p.product("w_xkv_2", 0, mem, keys)
        yield from p.product("w_xkv_2", COLS, mem, values, tokens_out=True)

    conv = None
    for _ in products():
        if conv is None and todo:
            conv = convolve(*todo.pop(0))
        if conv is not None and next(conv, "end") == "end":
            conv = None
    if conv is not None:
        run(conv)
    for c in todo:
        run(convolve(*c))

    i, psum, done = p.total(which=1)
    act.after(done, p.stat_read)
    mean = act.mark(act.q.activation(p.stat[:, 0, :], psum, ACT.Copy, scale=1.0 / D))
    p.bank.give(i, mean)
    mean_b = p.stat[:, 0:1, :].broadcast_to([P, CT, T])
    for g in range(CT):
        ug = u[:, g * CT:(g + 1) * CT, :]
        dve.after(u_ready[g], mean)
        u_ready[g] = dve.mark(dve.q.tensor_tensor(ug, ug, mean_b, ALU.subtract))
        p.add_squares(ug, u_ready[g], g)
    i, psum, done = p.total()
    root, ready = p.inverse_root(psum, done, p.stat[:, 1, :], 1.0 / D, 1)
    p.bank.give(i, root)
    rstd_b = p.stat[:, 1:2, :].broadcast_to([P, CT, T])
    for g in range(CT):
        ug = u[:, g * CT:(g + 1) * CT, :]
        dve.after(ready)
        done = dve.mark(dve.q.tensor_tensor(ug, ug, rstd_b, ALU.mult))
        i, tmp, free = p.scratch.take()
        act.after(done, free)
        for t in range(CT):
            k = g * CT + t
            s = act.mark(act.q.activation(tmp[:, t, :], u[:, k, :], ACT.Silu, scale=p.col("cc_ln_g", k),
                                          bias=p.col("cc_ln_b", k)))
        p.scratch.give(i, p.split_into(tmp, s, p.h, g * CT, CT))
    p.stat_read = done
    for b in range(CT):
        run(p.product("cc_w_out", b * COLS, p.h, p.residual(b, "cc_b_out")))


def mlp(p):
    dve, act = p.dve, p.act
    p.norm_x("norm2_g")
    ct = MLP_CHUNK // P
    mids = [Operand(p.mid.hi[:, i * ct:(i + 1) * ct, :], p.mid.lo[:, i * ct:(i + 1) * ct, :]) for i in range(2)]
    for m in mids:
        m.read = p.mid.read
    last = DFF // MLP_CHUNK - 1

    def squared_relu(mid, first):
        def evict(psum, mark):
            i, r, free = p.scratch.take()
            act.after(mark, free)
            relu = act.mark(act.q.activation(r, psum.rearrange("p (k t) -> p k t", t=T), ACT.Relu))
            act.after(relu)
            done = act.mark(act.q.activation(r, r, ACT.Square))
            p.scratch.give(i, p.split_into(r, done, mid, first, CT))
            return relu
        return evict

    for kind, c in mlp_order():
        mid = mids[c % 2]
        if kind == "up":
            for b in range(MLP_CHUNK // COLS):
                run(p.product("mlp_w1", c * MLP_CHUNK + b * COLS, p.h, squared_relu(mid, b * CT)))
        else:
            for b in range(CT):
                run(p.product("mlp_w2", b * COLS, mid, p.residual(b, sum_squares=c == last), row=c * MLP_CHUNK))


def renorm_x(p, gain, squares=True):
    ready = p.rms_scale()
    for g in range(CT):
        xg = p.x[:, g * CT:(g + 1) * CT, :]
        done = p.norm_group(xg, p.x_ready[g], gain, g, ready, xg, p.x_read[g])
        p.x_ready[g], p.x_read[g] = done, None
        if g == CT - 1:
            p.stat_read = done
    for g in range(CT):
        if squares:
            p.x_read[g] = p.add_squares(p.x[:, g * CT:(g + 1) * CT, :], p.x_ready[g], g)


def store_x(p):
    marks = []
    for g in range(CT):
        tiles = slice(g * CT, (g + 1) * CT)
        p.sp.after(p.x_ready[g])
        marks.append(p.dma(p.sp, p.dram["out"][tiles].rearrange("k p t -> p k t"), p.x[:, tiles, :], "x_stored"))
    p.sp.after(*marks)



def bias_rows(p):
    d, s = p.dram, p.phase_stack
    hot = p.sbuf("bucket_one_hot", [BUCKETS, BIAS_W], stack=s)
    neg = p.sbuf("bucket_neg", [NM, BIAS_W], stack=s)
    table = p.sbuf("rel_bias", [BUCKETS, NM], stack=s)
    landed = [p.dma(p.act, hot, d["bucket_one_hot"], "one_hot_landed"),
              p.dma(p.act, neg, d["bucket_neg"], "bias_neg_landed"),
              p.dma(p.act, table, d["rel_bias"], "rel_bias_landed")]
    i, bank, free = p.bank.take()
    rows = step(p.pe, [landed, free], lambda q: q.matmul(bank[0:NM, 0:BIAS_W], table, hot, start=True, stop=True))
    done = step(p.dve, [rows, landed], lambda q: q.tensor_tensor(neg, neg, bank[0:NM, 0:BIAS_W], ALU.add))
    p.bank.give(i, done)
    p.act.after(done)
    p.bias_rows_stored = p.dma(p.act, d["bias_rows"], neg.unsqueeze(1).broadcast_to([NM, P, BIAS_W]), "bias_rows_stored")


def gates(p, s):
    d, dve, act, pe = p.dram, p.dve, p.act, p.pe
    w, w_hi, w_lo = s.w_ba, s.w_ba_hi, s.w_ba_lo
    hi_done = step(act, [s.w_ba_landed], lambda q: q.activation(w_hi, w, ACT.Copy))
    lo_done = step(dve, [hi_done], lambda q: q.tensor_tensor(w_lo, w, w_hi.bitcast(F32), ALU.subtract))
    i, bank, free = p.bank.take()
    pe.after(free, hi_done, lo_done, p.h.ready)
    n = 2 * NG
    for t in range(TT):
        tok = slice(t * P, (t + 1) * P)
        for k in range(KT):
            for j, (x, y) in enumerate([(p.h.hi, w_hi), (p.h.lo, w_hi), (p.h.hi, w_lo)]):
                ins = pe.q.matmul(bank[:, t * n:(t + 1) * n], x[:, k, tok], y[:, k, :],
                                  start=k == 0 and j == 0, stop=k == KT - 1 and j == 2)
    made = pe.mark(ins)
    p.h.read = made
    psum = bank[:, 0:TT * n].rearrange("p (t n) -> p t n", t=TT)
    b_in, a_in = psum[:, :, 0:NG], psum[:, :, NG:n]
    sm = s.small
    e, ab, sp = sm[:, 0], sm[:, 1], sm[:, 2]
    read_b = m1 = step(act, [made], lambda q: q.activation(s.beta, b_in, ACT.Exp, scale=-1.0))
    m1 = step(dve, [m1], lambda q: q.tensor_scalar(s.beta, s.beta, 1.0, None, ALU.add))
    beta = step(dve, [m1], lambda q: q.reciprocal(s.beta, s.beta))
    m2 = step(dve, [read_b, s.heads_landed], lambda q: q.tensor_tensor(
        e, a_in, s.dt_bias.unsqueeze(1).broadcast_to([P, TT, NG]), ALU.add))
    p.bank.give(i, m1, m2)
    m3 = step(act, [m2], lambda q: q.activation(ab, e, ACT.Abs))
    m4 = step(act, [m3], lambda q: q.activation(ab, ab, ACT.Exp, scale=-1.0))
    m4 = step(act, [m4], lambda q: q.activation(ab, ab, ACT.Ln, bias=p.m("ones")[:, 0:1]))
    m5 = step(dve, [m4], lambda q: q.scalar_tensor_tensor(out=sp, in0=e, scalar=0.0, in1=ab, op0=ALU.max, op1=ALU.add))
    m6 = step(act, [s.heads_landed], lambda q: q.activation(s.a_log, s.a_log, ACT.Exp))
    g_done = step(dve, [m5, m6], lambda q: q.scalar_tensor_tensor(
        out=s.g, in0=sp, scalar=-1.0, in1=s.a_log.unsqueeze(1).broadcast_to([P, TT, NG]), op0=ALU.mult, op1=ALU.mult))
    i, bank, free = p.bank.take()
    pe.after(g_done, free)
    for t in range(TT):
        pe.q.matmul(bank[:, t * NG:(t + 1) * NG], p.m("cumsum"), s.g[:, t, :], start=True, stop=True)
        ins = pe.q.matmul(bank[:, (TT + t) * NG:(TT + t + 1) * NG], p.m("same_chunk"), s.g[:, t, :], start=True, stop=True)
    sums = pe.mark(ins)
    upto = bank[:, 0:TT * NG].rearrange("p (t n) -> p t n", t=TT)
    whole = bank[:, TT * NG:2 * TT * NG].rearrange("p (t n) -> p t n", t=TT)
    c1 = step(dve, [sums], lambda q: q.tensor_copy(s.cum, upto))
    c2 = step(dve, [c1], lambda q: q.tensor_tensor(s.k_decay, whole, s.cum, ALU.subtract))
    c3 = step(act, [c2], lambda q: q.activation(s.k_decay, s.k_decay, ACT.Exp))
    c4 = step(act, [c1], lambda q: q.activation(s.beta_decay, s.cum, ACT.Exp))
    p.bank.give(i, c1, c2)
    c5 = step(dve, [c4, beta], lambda q: q.tensor_tensor(s.beta_decay, s.beta_decay, s.beta, ALU.mult))
    s.gates_ready = [beta, g_done, c1, c3, c5]


def conv_silu(p, s, g, part, out, free):
    dve, act = p.dve, p.act

    def evict(psum, mark):
        i, pad, pad_free = s.pad.take()
        copied = step(act, [mark, pad_free], lambda q: q.activation(
            pad[:, :, GDN_K - 1:], psum.rearrange("p (k t) -> p k t", t=T), ACT.Copy))
        dst = out() if callable(out) else out
        done = [None] * CT
        for j in range(GDN_K):
            for t in range(CT):
                w = p.col("gdn_conv_w_2", (part * NG + g * CT + t) * GDN_K + j)
                tap = pad[:, t, j:j + T]
                if j == 0:
                    done[t] = step(dve, [copied, free], lambda q: q.tensor_scalar(dst[:, t, :], tap, w, None, ALU.mult))
                else:
                    done[t] = step(dve, [done[t]], lambda q: q.scalar_tensor_tensor(
                        out=dst[:, t, :], in0=tap, scalar=w, in1=dst[:, t, :], op0=ALU.mult, op1=ALU.add))
        s.pad.give(i, done[-1])
        s.conv_ready[g, part] = step(act, [done], lambda q: q.activation(dst, dst, ACT.Silu))
        return copied
    return evict


def l2_normalise(p, x, ready, scale, eps):
    i, sq, free = p.scratch.take()
    squared = step(p.act, [ready, free], lambda q: q.activation(sq, x, ACT.Square))
    flat = sq.rearrange("p k t -> p (k t)")
    done = None
    yield None
    for half in range(2):
        cols = slice(half * 512, (half + 1) * 512)
        bi, bank, bfree = p.bank.take()
        summed = step(p.pe, [squared, bfree], lambda q: q.matmul(bank, p.m("ones"), flat[:, cols], start=True, stop=True))
        root = step(p.act, [summed], lambda q: q.activation(flat[:, cols], bank, ACT.Sqrt, bias=p.eps[:, eps:eps + 1], scale=scale))
        p.bank.give(bi, root)
        inv = step(p.dve, [root], lambda q: q.reciprocal(flat[:, cols], flat[:, cols]))
        xs = x.rearrange("p k t -> p (k t)")[:, cols]
        done = step(p.dve, [inv], lambda q: q.tensor_tensor(xs, xs, flat[:, cols], ALU.mult))
        yield None
    p.scratch.give(i, done)
    yield done


def head_norm(p, o, ready, gain, gate=None, gate_ready=None):
    i, sq, free = p.scratch.take()
    squared = step(p.act, [ready, free], lambda q: q.activation(sq, o, ACT.Square))
    yield None
    flat, of = sq.rearrange("p k t -> p (k t)"), o.rearrange("p k t -> p (k t)")
    for half in range(2):
        cols = slice(half * 512, (half + 1) * 512)
        bi, bank, bfree = p.bank.take()
        summed = step(p.pe, [squared, bfree], lambda q: q.matmul(bank, p.m("ones"), flat[:, cols], start=True, stop=True))
        root = step(p.act, [summed], lambda q: q.activation(flat[:, cols], bank, ACT.Sqrt, bias=p.eps[:, 0:1], scale=1.0 / HD))
        p.bank.give(bi, root)
        inv = step(p.dve, [root], lambda q: q.reciprocal(flat[:, cols], flat[:, cols]))
        done = step(p.dve, [inv], lambda q: q.scalar_tensor_tensor(
            out=of[:, cols], in0=of[:, cols], scalar=p.col(gain, 0), in1=flat[:, cols], op0=ALU.mult, op1=ALU.mult))
        if gate is not None:
            gf = gate.rearrange("p k t -> p (k t)")[:, cols]
            done = step(p.dve, [done, gate_ready], lambda q: q.tensor_tensor(of[:, cols], of[:, cols], gf, ALU.mult))
        yield None
    p.scratch.give(i, done)
    yield done


def transposes(p, dst_bank, blocks):
    for n, b in enumerate(blocks):
        ins = p.pe.q.transpose(dst_bank[:, n * P:(n + 1) * P], b, p.m("identity"))
    return p.pe.mark(ins)


def delta_rule(p, s, g):
    pe, dve, act, pool = p.pe, p.dve, p.act, p.pool
    qt, kt, vb, z = s.q_t[g], s.k_t[g], s.v_beta[g], s.z[g]
    heads = range(CT)
    hs = slice(g * CT, (g + 1) * CT)
    four = lambda ap: ap.unsqueeze(1).broadcast_to([P, CT, P])
    bank4 = lambda b: b.rearrange("p (h n) -> p h n", h=CT)

    def row(t):
        return slice(t * P, (t + 1) * P)

    q_ready = k_ready = None
    for q_ready in l2_normalise(p, qt, s.conv_ready[g, 0], float(HD), 2):
        yield
    for k_ready in l2_normalise(p, kt, s.conv_ready[g, 1], 1.0, 0):
        yield

    decay_ready, ei, (eg_i, eg, eg_free) = [None] * TT, None, p.scratch.take()
    for t in range(TT):
        gi, gb, gfree = p.scratch.take()
        spread = step(dve, [s.gates_ready, gfree], lambda q: q.tensor_copy(
            gb[:, :, 0:P], s.g[:, t, hs].unsqueeze(2).broadcast_to([P, CT, P])))
        bi, bank, bfree = p.bank.take()
        pe.after(spread, bfree)
        for h in heads:
            ins = pe.q.matmul(bank[:, row(h)], gb[:, h, 0:P], p.m("cumsum"), start=True, stop=True)
        rows = pe.mark(ins)
        p.scratch.give(gi, rows)
        d = s.decay[t]
        free = s.mem_read["decay", t]
        grown = step(act, [rows, eg_free], lambda q: q.activation(eg[:, :, row(t)], bank4(bank), ACT.Exp))
        diff = step(dve, [rows, free, grown], lambda q: q.tensor_tensor(d, four(p.m("causal_neg")), bank4(bank), ALU.subtract))
        p.bank.give(bi, grown, diff)
        for h in heads:
            decay_ready[t] = step(act, [diff], lambda q: q.activation(
                d[:, h, :], d[:, h, :], ACT.Exp, bias=s.cum[:, t, g * CT + h:g * CT + h + 1]))
        yield

    a_t_ready, qk_ready = [None] * TT, [None] * TT
    for t in range(TT):
        a, at, d = s.a[t], s.a_t[t], s.decay[t]
        bi, bank, bfree = p.bank.take()
        pe.after(k_ready, bfree)
        for h in heads:
            ins = pe.q.matmul(bank[:, row(h)], kt[:, h, row(t)], kt[:, h, row(t)], start=True, stop=True)
        kk = pe.mark(ins)
        for h in heads:
            made = step(dve, [kk, decay_ready[t], s.mem_read["a", t]], lambda q: q.scalar_tensor_tensor(
                out=a[:, h, :], in0=bank[:, row(h)], scalar=s.beta[:, t, g * CT + h:g * CT + h + 1],
                in1=d[:, h, :], op0=ALU.mult, op1=ALU.mult))
        p.bank.give(bi, made)
        s.a_ready[t] = made
        bi, bank, bfree = p.bank.take()
        pe.after(q_ready, bfree)
        for h in heads:
            ins = pe.q.matmul(bank[:, row(h)], qt[:, h, row(t)], kt[:, h, row(t)], start=True, stop=True)
        qk = pe.mark(ins)
        i, tmp, free = p.scratch.take()
        scaled = step(dve, [qk, free], lambda q: q.tensor_tensor(tmp[:, :, 0:P], bank4(bank), d, ALU.mult))
        p.bank.give(bi, scaled)
        yield
        bi, bank, bfree = p.bank.take()
        pe.after(made, bfree)
        turned = transposes(p, bank, [a[:, h, :] for h in heads])
        a_t_ready[t] = step(act, [turned, s.mem_read["a_t", t]], lambda q: q.activation(at, bank4(bank), ACT.Copy))
        p.bank.give(bi, a_t_ready[t])
        bi, bank, bfree = p.bank.take()
        pe.after(scaled, bfree)
        turned = transposes(p, bank, [tmp[:, h, 0:P] for h in heads])
        p.scratch.give(i, turned)
        qk_ready[t] = step(act, [turned, s.mem_read["qk_t", t]], lambda q: q.activation(s.qk_t[t], bank4(bank), ACT.Copy))
        p.bank.give(bi, qk_ready[t])
        yield
    grown_q = step(dve, [qk, grown], lambda q: q.tensor_tensor(qt, qt, eg, ALU.mult))
    ends = eg.rearrange("p h (c i) -> p h c i", i=CHUNK)[:, :, :, CHUNK - 1]
    last_ready = step(dve, [grown, s.mem_read["last", 0]], lambda q: q.tensor_copy(s.last, ends))
    p.scratch.give(eg_i, grown_q, last_ready)

    inv_ready, u_ready = [None] * TT, [None] * TT
    for t in range(TT):
        a, at, u = s.a[t], s.a_t[t], s.u[t]
        for src, mask, out, ready in ((at, "merge1_t", u, u_ready), (a, "merge1", a, inv_ready)):
            m1 = step(dve, [a_t_ready[t], s.a_ready[t], s.mem_read["u", t]],
                      lambda q: q.tensor_tensor(out, src, four(p.m(mask)), ALU.mult))
            ready[t] = step(dve, [m1], lambda q: q.scalar_tensor_tensor(
                out=out, in0=out, scalar=-1.0, in1=four(p.m("identity")), op0=ALU.mult, op1=ALU.add))
    yield
    y_read = [decay_ready[t] for t in range(TT)]
    for n in range(2, 7):
        y_done, off_i = [None] * TT, [None] * TT
        for t in range(TT):
            at, inv, y = s.a_t[t], s.a[t], s.decay[t]
            i, off, free = p.scratch.take()
            masked = step(pool, [a_t_ready[t], free], lambda q: q.tensor_tensor(
                off[:, :, 0:P], at, four(p.m(f"merge{n}_t")), ALU.mult))
            bi, bank, bfree = p.bank.take()
            pe.after(masked, inv_ready[t], bfree)
            for h in heads:
                ins = pe.q.matmul(bank[:, row(h)], off[:, h, 0:P], inv[:, h, :], start=True, stop=True)
            made = pe.mark(ins)
            p.scratch.give(i, made)
            y_done[t] = step(act, [made, y_read[t], scaled], lambda q: q.activation(y, bank4(bank), ACT.Copy))
            p.bank.give(bi, y_done[t])
        yield
        for t in range(TT):
            inv, u, y = s.a[t], s.u[t], s.decay[t]
            if n < 6:
                bi, bank, bfree = p.bank.take()
                pe.after(y_done[t], u_ready[t], bfree)
                for h in heads:
                    ins = pe.q.matmul(bank[:, row(h)], u[:, h, :], y[:, h, :], start=True, stop=True)
                made = pe.mark(ins)
                inv_ready[t] = step(dve, [made], lambda q: q.tensor_tensor(inv, inv, bank4(bank), ALU.subtract))
                p.bank.give(bi, inv_ready[t])
            bi, bank, bfree = p.bank.take()
            pe.after(y_done[t], u_ready[t], bfree)
            for h in heads:
                ins = pe.q.matmul(bank[:, row(h)], y[:, h, :], u[:, h, :], start=True, stop=True)
            y_read[t] = made = pe.mark(ins)
            u_ready[t] = step(dve, [made], lambda q: q.tensor_tensor(u, u, bank4(bank), ALU.subtract))
            p.bank.give(bi, u_ready[t])
        yield

    kb_i, kb, kb_free = p.scratch.take()
    kb = kb.rearrange("p k t -> p (k t)").rearrange("p (t h n) -> p t h n", t=TT, h=CT)
    kb_ready, kd_ready = [None] * TT, [None] * TT
    for t in range(TT):
        bi, bank, bfree = p.bank.take()
        pe.after(k_ready, bfree)
        turned = transposes(p, bank, [kt[:, h, row(t)] for h in heads])
        for h in heads:
            c = g * CT + h
            kb_ready[t] = step(act, [turned, kb_free], lambda q: q.activation(
                kb[:, t, h, :], bank[:, row(h)], ACT.Copy, scale=s.beta_decay[:, t, c:c + 1]))
        for h in heads:
            c = g * CT + h
            kd_ready[t] = step(dve, [kb_ready[t], y_read[t]], lambda q: q.tensor_scalar(
                s.decay[t][:, h, :], bank[:, row(h)], s.k_decay[:, t, c:c + 1], None, ALU.mult))
        p.bank.give(bi, kb_ready[t], kd_ready[t])
        yield

    v_ready, w_ready = [None] * TT, [None] * TT
    for t in range(TT):
        u, w, v = s.u[t], s.a_t[t], s.a[t]
        bi, bank, bfree = p.bank.take()
        pe.after(u_ready[t], s.v_ready[g], bfree)
        for h in heads:
            ins = pe.q.matmul(bank[:, row(h)], u[:, h, :], vb[:, t, h, :], start=True, stop=True)
        made = pe.mark(ins)
        v_ready[t] = step(act, [made], lambda q: q.activation(v, bank4(bank), ACT.Copy))
        p.bank.give(bi, v_ready[t])
        bi, bank, bfree = p.bank.take()
        pe.after(kb_ready[t], bfree)
        for h in heads:
            ins = pe.q.matmul(bank[:, row(h)], kb[:, t, h, :], u[:, h, :], start=True, stop=True)
        made = pe.mark(ins)
        w_ready[t] = step(act, [made], lambda q: q.activation(w, bank4(bank), ACT.Copy))
        p.bank.give(bi, w_ready[t])
    p.scratch.give(kb_i, made)
    yield

    o, state = s.o[g], s.state
    state_ready = o_ready = None
    for c in range(T // CHUNK):
        t, half = divmod(c, TT)
        r = slice(half * CHUNK, (half + 1) * CHUNK)
        tok = slice(c * CHUNK, (c + 1) * CHUNK)
        v, w, kd, qk = s.a[t], s.a_t[t], s.decay[t], s.qk_t[t]
        if c > 0:
            bi, bank, bfree = p.bank.take()
            pe.after(state_ready, w_ready[t], bfree)
            for h in heads:
                ins = pe.q.matmul(bank[r, row(h)], w[:, h, r], state[:, h, :], start=True, stop=True)
            made = pe.mark(ins)
            new = step(dve, [made, v_ready[t]], lambda q: q.tensor_tensor(v[r], v[r], bank4(bank)[r], ALU.subtract))
            p.bank.give(bi, new)
            yield
        else:
            new = v_ready[t]
        if c < T // CHUNK - 1:
            bi, bank, bfree = p.bank.take()
            pe.after(new, kd_ready[t], bfree)
            for h in heads:
                ins = pe.q.matmul(bank[:, row(h)], kd[r, h, :], v[r, h, :], start=True, stop=True)
            made = pe.mark(ins)
            grown_bank, grown_i = bank, bi
        oi, obank, ofree = p.bank.take()
        pe.after(grown_q, qk_ready[t], new, ofree)
        for h in heads:
            out = obank[:, h * CHUNK:(h + 1) * CHUNK]
            if c > 0:
                pe.q.matmul(out, state[:, h, :], qt[:, h, tok], start=True, stop=False)
            ins = pe.q.matmul(out, v[r, h, :], qk[r, h, r], start=c == 0, stop=True)
        o_made = pe.mark(ins)
        if c < T // CHUNK - 1:
            if c == 0:
                state_ready = step(dve, [made, s.mem_read["state", 0]], lambda q: q.tensor_copy(state, bank4(grown_bank)))
            else:
                for h in heads:
                    state_ready = step(dve, [o_made], lambda q: q.scalar_tensor_tensor(
                        out=state[:, h, :], in0=state[:, h, :], scalar=s.last[:, h, c:c + 1],
                        in1=grown_bank[:, row(h)], op0=ALU.mult, op1=ALU.add))
            p.bank.give(grown_i, state_ready)
        o_ready = step(act, [o_made], lambda q: q.activation(
            o[:, :, tok], obank[:, 0:CT * CHUNK].rearrange("p (h n) -> p h n", h=CT), ACT.Copy))
        p.bank.give(oi, o_ready)
        yield
    for name in ("decay", "a", "a_t", "qk_t", "u"):
        for t in range(TT):
            s.mem_read[name, t] = o_made
    s.mem_read["state", 0] = o_made
    s.mem_read["last", 0] = state_ready
    s.inputs_read[g] = o_made

    for s.o_ready[g] in head_norm(p, o, o_ready, "gdn_norm_g_2", z, s.z_ready[g]):
        yield
    s.inputs_read[g] = [o_made, s.o_ready[g]]


def attention_head(p, q_t, k_t, v, ready, out, out_free, scale, tiles, bias, small, state):
    pe, dve, act = p.pe, p.dve, p.act
    width = [n * P for n in tiles]
    at = [0, width[0]]
    total = sum(width)
    neg_max, total_p, inv = small[:, 0, :], small[:, 1, :], small[:, 2, :]
    i, buf, free = p.scratch.take()
    flat = buf.rearrange("p k t -> p (k t)")
    e, p_t = flat[:, 0:512], flat[:, 512:1024]
    bi, bank, bfree = p.bank.take()
    pe.after(ready, bfree)
    for t in range(TT):
        ins = pe.q.matmul(bank[:, at[t]:at[t] + width[t]], q_t[:, t * P:(t + 1) * P], k_t[:, 0:width[t]], start=True, stop=True)
    scores = pe.mark(ins)
    yield
    if bias is not None:
        added = bias(bank, e, [scores, free], scale, at, width)
        p.bank.give(bi, added)
        src, scale_in, src_ready = e, 1.0, added
    else:
        src, scale_in, src_ready = bank, scale, scores
    for t in range(TT):
        m1 = step(dve, [src_ready], lambda q: q.tensor_reduce(neg_max[:, t:t + 1], src[:, at[t]:at[t] + width[t]], AX.X, ALU.max))
    m1 = step(dve, [m1], lambda q: q.tensor_scalar(neg_max, neg_max, -scale_in, None, ALU.mult))
    for t in range(TT):
        seg = slice(at[t], at[t] + width[t])
        ex = step(act, [m1, free], lambda q: q.activation(e[:, seg], src[:, seg], ACT.Exp, bias=neg_max[:, t:t + 1],
                                                          scale=scale_in, accum_out=total_p[:, t:t + 1]))
    if bias is None:
        p.bank.give(bi, ex)
    m2 = step(dve, [ex], lambda q: q.reciprocal(inv, total_p))
    for t in range(TT):
        seg = slice(at[t], at[t] + width[t])
        m3 = step(dve, [m2], lambda q: q.tensor_scalar(e[:, seg], e[:, seg], inv[:, t:t + 1], None, ALU.mult))
    yield
    blocks = [(t, k) for k in range(max(tiles)) for t in range(TT) if k < tiles[t]]
    bi, bank, bfree = p.bank.take()
    pe.after(m3, bfree)
    turned = transposes(p, bank, [e[:, at[t] + k * P:at[t] + (k + 1) * P] for t, k in blocks])
    c = step(act, [turned], lambda q: q.activation(p_t[:, 0:total], bank[:, 0:total], ACT.Copy))
    p.bank.give(bi, c)
    yield
    bi, bank, bfree = p.bank.take()
    pe.after(c, bfree)
    for k in range(max(tiles)):
        mine = [n for n, (t, kk) in enumerate(blocks) if kk == k]
        first_t = blocks[mine[0]][0]
        ins = pe.q.matmul(bank[:, first_t * P:T], v[k], p_t[:, mine[0] * P:(mine[-1] + 1) * P],
                          start=k == 0, stop=k == max(tiles) - 1, skip_group_check=True)
    made = pe.mark(ins)
    p.scratch.give(i, made)
    done = step(act, [made, out_free], lambda q: q.activation(out, bank[:, 0:T], ACT.Copy))
    p.bank.give(bi, done)
    state.append(done)
    yield


def pipeline(generators, depth, beside=None):
    waiting, live = list(generators), []
    while waiting or live:
        if waiting and len(live) < depth:
            live.append(waiting.pop(0))
        live = [x for x in live if next(x, "end") != "end"]
        if beside is not None:
            next(beside, None)


class MixerMemory:
    pass


def mixer(p):
    d, dve, act, pe, stack = p.dram, p.dve, p.act, p.pe, p.phase_stack
    s = MixerMemory()
    sb = lambda name, shape, dt=F32: p.sbuf(name, shape, dt, stack)
    s.w_ba_hi, s.w_ba_lo = sb("w_ba_hi", [P, KT, 16], F32R), sb("w_ba_lo", [P, KT, 16], F32R)
    s.dt_bias, s.a_log = sb("dt_bias", [P, NG]), sb("a_log", [P, NG])
    s.beta, s.g, s.cum, s.k_decay, s.beta_decay = (sb(n, [P, TT, NG]) for n in ("beta", "log_decay", "cum", "k_decay", "beta_decay"))
    s.small = sb("gate_small", [P, 3, TT, NG])
    inputs = [sb(f"heads{g}", [P, 4, CT, T]) for g in range(2)]
    s.q_t, s.k_t, s.z = ([x[:, n] for x in inputs] for n in range(3))
    s.v_beta = [x[:, 3].rearrange("p k t -> p (k t)").rearrange("p (t h n) -> p t h n", t=TT, h=CT) for x in inputs]
    s.o = [sb(f"delta_out{g}", [P, CT, T]) for g in range(2)]
    s.w_ba = s.o[1].rearrange("p k t -> p (k t)")[:, 0:KT * 2 * NG].rearrange("p (k n) -> p k n", k=KT)
    work = sb("delta_work", [P, 5, TT, CT, P])
    s.decay, s.a, s.a_t, s.u, s.qk_t = ([work[:, n, t] for t in range(TT)] for n in range(5))
    s.state, s.last = sb("state", [P, CT, HD]), sb("last_decay", [P, CT, T // CHUNK])
    s.pad = Ring([sb("conv_pad", [P, CT, GDN_K - 1 + T])])
    v_own = sb("moba_v", [P, TT, NM * HD])
    small = sb("softmax_small", [P, NM, 3, TT])
    s.mem_read = {(n, t): None for n in ("decay", "a", "a_t", "u", "qk_t", "state", "last") for t in range(TT)}
    s.conv_ready, s.a_ready, s.inputs_read = {}, [None] * TT, [None] * 2
    s.v_ready, s.z_ready, s.o_ready = [None] * 2, [None] * 2, [None] * 2

    s.w_ba_landed = p.dma(act, s.w_ba, d["w_in_2"][:, 4 * GW:4 * GW + 16].rearrange("(k p) n -> p k n", p=P), "w_ba_landed")
    p.dma(act, s.dt_bias, d["dt_bias"].partition_broadcast(P), "heads_landed")
    s.heads_landed = p.dma(act, s.a_log, d["a_log"].partition_broadcast(P), "heads_landed")
    s.pad.give(0, step(p.pool, [], lambda q: q.memset(s.pad.buffers[0][:, :, 0:GDN_K - 1], 0.0)))

    p.norm_x("mix_norm_g_2")
    gates(p, s)

    def v_block(g):
        held = {}

        def out():
            i, buf, free = p.scratch.take()
            held["i"] = i
            dve.after(free)
            return buf
        conv = conv_silu(p, s, g, 2, out, None)

        def evict(psum, mark):
            copied = conv(psum, mark)
            v = p.scratch.buffers[held["i"]]
            turned_list = []
            s.pending.append((g, held["i"], v))
            return copied
        return evict

    def turn_v(g, i, v):
        for t in range(TT):
            bi, bank, bfree = p.bank.take()
            pe.after(s.conv_ready[g, 2], bfree)
            turned = transposes(p, bank, [v[:, h, t * P:(t + 1) * P] for h in range(CT)])
            for h in range(CT):
                c = g * CT + h
                done = step(act, [turned, s.gates_ready], lambda q: q.activation(
                    s.v_beta[g][:, t, h, :], bank[:, h * P:(h + 1) * P], ACT.Copy, scale=s.beta[:, t, c:c + 1]))
            p.bank.give(bi, done)
        p.scratch.give(i, turned)
        s.v_ready[g] = done

    def z_block(g):
        def evict(psum, mark):
            s.z_ready[g] = step(act, [mark], lambda q: q.activation(
                s.z[g], psum.rearrange("p (k t) -> p k t", t=T), ACT.Silu))
            return s.z_ready[g]
        return evict

    def copy_out(dst, free, key):
        def evict(psum, mark):
            done = step(act, [mark, free()], lambda q: q.activation(dst, psum.rearrange(
                "p (k t) -> p k t", k=dst.shape[1]), ACT.Copy))
            moba_ready[key] = done
            return done
        return evict

    s.pending = []
    moba_ready = {}
    mq = inputs[0][:, 0:2].rearrange("p a k t -> p (a k) t")
    mk = inputs[0][:, 2:4].rearrange("p a k t -> p (a k) t")

    def products():
        for g in range(2):
            yield from p.product("w_in_2", g * COLS, p.h, conv_silu(p, s, g, 0, s.q_t[g], None))
            yield from p.product("w_in_2", GW + g * COLS, p.h, conv_silu(p, s, g, 1, s.k_t[g], None))
            yield from p.product("w_in_2", 2 * GW + g * COLS, p.h, v_block(g))
            yield from p.product("w_in_2", 3 * GW + g * COLS, p.h, z_block(g))
        base = 4 * GW + 2 * NG
        for b in range(6):
            if b < 4:
                dst = (mq, mk)[b // 2][:, (b % 2) * CT:(b % 2 + 1) * CT, :]
                yield from p.product("w_in_2", base + b * COLS, p.h, copy_out(dst, lambda: s.inputs_read[0], b))
            else:
                half = v_own[:, :, (b - 4) * COLS:(b - 3) * COLS]
                yield from p.product("w_in_2", base + b * COLS, p.h, copy_out(half, lambda: None, b), tokens_out=True)

    side = None
    started = 0
    for _ in products():
        if s.pending:
            turn_v(*s.pending.pop(0))
        if side is None and started < 2 and s.z_ready[started] is not None:
            side = delta_rule(p, s, started)
            started += 1
        if side is not None and next(side, "end") == "end":
            side = None
    if side is not None:
        run(side)
    while started < 2:
        run(delta_rule(p, s, started))
        started += 1

    for g in range(2):
        p.split_into(s.o[g], s.o_ready[g], p.h, g * CT, CT)
    bias_sb = work[:, 0:2].rearrange("p a t h n -> p (a t h n)").rearrange("p (h j) -> p h j", h=NM)
    act.after(s.mem_read["decay", 0], s.mem_read["a", 0], p.bias_rows_stored)
    skew = bass.AP(d["bias_rows"].tensor, P - 1, [[BIAS_W - 1, P], [P * BIAS_W, NM], [1, T]])
    bias_landed = p.dma(act, bias_sb, skew, "bias_landed")
    o_b = work[:, 2:4].rearrange("p a t h n -> p (a t h n)").rearrange("p (h j) -> p h j", h=NM)
    heads_done = []

    def moba_bias(h):
        def add(bank, e, marks, scale, at, width):
            m1 = step(dve, [marks, bias_landed], lambda q: q.scalar_tensor_tensor(
                out=e[:, 0:P], in0=bank[:, 0:P], scalar=scale, in1=bias_sb[:, h, P:T], op0=ALU.mult, op1=ALU.add))
            return step(dve, [marks, m1], lambda q: q.scalar_tensor_tensor(
                out=e[:, P:P + T], in0=bank[:, P:P + T], scalar=scale, in1=bias_sb[:, h, :], op0=ALU.mult, op1=ALU.add))
        return add

    def one(h):
        cols = slice(h * HD, (h + 1) * HD)
        ready = [moba_ready[h // CT], moba_ready[2 + h // CT], moba_ready[4 + h // CT]]
        return attention_head(p, mq[:, h, :], mk[:, h, :], [v_own[:, 0, cols], v_own[:, 1, cols]], ready,
                              o_b[:, h, :], s.mem_read["u", 0], HD ** -0.5, [1, 2], moba_bias(h), small[:, h], heads_done)

    pipeline([one(h) for h in range(NM)], 3)
    for g in range(2):
        ob = o_b[:, g * CT:(g + 1) * CT, :]
        for done in head_norm(p, ob, heads_done, "moba_norm_g_2"):
            pass
        p.split_into(ob, done, p.h, (2 + g) * CT, CT)
    for b in range(CT):
        run(p.product("w_out_2", b * COLS, p.h, p.residual(b)))



def cross_attention(p):
    stack, act = p.phase_stack, p.act
    q_t = p.sbuf("cross_q", [P, NX, T], stack=stack)
    o = p.sbuf("cross_out", [P, NX, T], stack=stack)
    small = p.sbuf("cross_small", [P, NX, 3, TT], stack=stack)
    x_o = Operand(p.mid.hi[:, 0:NX, :], p.mid.lo[:, 0:NX, :])
    p.norm_x("xattn_norm_g_2")
    ready = []

    def evict(psum, mark):
        ready.append(step(act, [mark], lambda q: q.activation(q_t, psum.rearrange("p (k t) -> p k t", t=T), ACT.Copy)))
        return ready[-1]
    run(p.product("w_xq_2", 0, p.h, evict))
    done = []

    def one(h):
        cols = slice(h * HD, (h + 1) * HD)
        return attention_head(p, q_t[:, h, :], p.mem_k[:, h, :], [p.mem_v[:, 0, cols], p.mem_v[:, 1, cols]],
                              [ready, p.mem_k_ready, p.mem_v_ready], o[:, h, :], None, HD ** -0.5, [2, 2], None,
                              small[:, h], done)
    pipeline([one(h) for h in range(NX)], 3)
    p.split_into(o, done, x_o, 0, NX)
    for b in range(CT):
        run(p.product("w_xo_2", b * COLS, x_o, p.residual(b)))
    p.mid.read = x_o.read


def conv_ffn(p):
    dve, act, stack = p.dve, p.act, p.phase_stack
    pads = Ring([p.sbuf(f"ffn_pad{i}", [P, CT, FFN_K - 1 + T], stack=stack) for i in range(2)])
    gate = Ring([p.sbuf(f"ffn_gate{i}", [P, CT, T], stack=stack) for i in range(2)])
    for i in range(2):
        pads.give(i, step(p.pool, [], lambda q: q.memset(pads.buffers[i][:, :, 0:FFN_K - 1], 0.0)))
    p.norm_x("ffn_norm_g_2")
    mids = [Operand(p.mid.hi[:, i * CT:(i + 1) * CT, :], p.mid.lo[:, i * CT:(i + 1) * CT, :]) for i in range(3)]
    for m in mids:
        m.read = p.mid.read
    gates_ready = {}

    def evict_gate(c):
        def evict(psum, mark):
            i, pad, free = pads.take()
            copied = step(act, [mark, free], lambda q: q.activation(
                pad[:, :, FFN_K - 1:], psum.rearrange("p (k t) -> p k t", t=T), ACT.Copy))
            gi, g, gfree = gate.take()
            done = [None] * CT
            for j in range(FFN_K):
                for t in range(CT):
                    w = p.col("ffn_conv_w_2", (c * CT + t) * FFN_K + j)
                    tap = pad[:, t, j:j + T]
                    if j == 0:
                        b = p.col("ffn_conv_b_2", c * CT + t)
                        done[t] = step(dve, [copied, gfree], lambda q: q.tensor_scalar(g[:, t, :], tap, w, b, ALU.mult, ALU.add))
                    else:
                        done[t] = step(dve, [done[t]], lambda q: q.scalar_tensor_tensor(
                            out=g[:, t, :], in0=tap, scalar=w, in1=g[:, t, :], op0=ALU.mult, op1=ALU.add))
            pads.give(i, done[-1])
            gates_ready[c] = (gi, g, step(act, [done], lambda q: q.activation(g, g, ACT.Silu)))
            return copied
        return evict

    def evict_up(c, mid):
        def evict(psum, mark):
            gi, g, g_done = gates_ready[c]
            made = step(dve, [mark, g_done], lambda q: q.tensor_tensor(g, g, psum.rearrange("p (k t) -> p k t", t=T), ALU.mult))
            gate.give(gi, p.split_into(g, made, mid, 0, CT))
            return made
        return evict

    last = DFF2 // COLS - 1
    for kind, c in ffn_order():
        mid = mids[c % 3]
        if kind == "up":
            run(p.product("w_gate_2", c * COLS, p.h, evict_gate(c)))
            run(p.product("w_up_2", c * COLS, p.h, evict_up(c, mid)))
        else:
            for b in range(CT):
                run(p.product("w_down_2", b * COLS, mid, p.residual(b, sum_squares=c == last), row=c * COLS))



STAGES = 3


def build(nc, dram):
    with ExitStack() as stack:
        p = Program(nc, stack, dram)
        p.plan_weights()
        p.pool_every = 2
        p.constants()
        with ExitStack() as p.phase_stack:
            bias_rows(p)
            conformer(p)
            p.pool_every = 0
            mlp(p)
            renorm_x(p, "final_g", STAGES > 1)
        if STAGES > 1:
            with ExitStack() as p.phase_stack:
                p.phase()
                p.pool_every = 2
                mixer(p)
        if STAGES > 2:
            with ExitStack() as p.phase_stack:
                p.phase()
                p.pool_every = 0
                p.mid = Operand(p.sbuf("mid_hi", [P, KT, T], F32R, p.phase_stack), p.sbuf("mid_lo", [P, KT, T], F32R, p.phase_stack))
                cross_attention(p)
                conv_ffn(p)
                renorm_x(p, "final_norm_g_2", squares=False)
        store_x(p)



WEIGHTS = ["cc_w_in", "cc_w_out", "mlp_w1", "mlp_w2", "w_in_2", "w_out_2", "w_xq_2", "w_xkv_2", "w_xo_2",
           "w_gate_2", "w_up_2", "w_down_2"]


def layout(inputs):
    a = {}
    for name, key in (("x", "x"), ("mem", "mem_2")):
        a[name] = np.ascontiguousarray(np.asarray(inputs[key])[0].T.reshape(KT, P, T))
    for name in WEIGHTS:
        w = np.asarray(inputs[name])
        a[name] = np.ascontiguousarray(w[0])
    parts = []
    for name, tiles in VECTORS:
        parts.append(np.asarray(inputs[name]).reshape(tiles, P).T)
    for name, tiles, taps in FILTERS:
        parts.append(np.asarray(inputs[name]).reshape(taps, tiles, P).transpose(2, 1, 0).reshape(P, tiles * taps))
    a["feature_columns"] = np.ascontiguousarray(np.concatenate(parts, axis=1))
    a["masks"] = np.ascontiguousarray(masks())
    hot, neg = bucket_rows()
    a["bucket_one_hot"], a["bucket_neg"] = hot, neg
    a["rel_bias"] = np.ascontiguousarray(np.asarray(inputs["rel_bias_2"]))
    a["a_log"] = np.ascontiguousarray(np.asarray(inputs["gdn_a_log_2"]))
    a["dt_bias"] = np.ascontiguousarray(np.asarray(inputs["gdn_dt_bias_2"]))
    return a


def kernel(**inputs):
    import concourse.bacc as bacc
    from concourse.bass_utils import run_bass_kernel_spmd

    nc = bacc.Bacc("TRN2", target_bir_lowering=False, num_devices=1)
    arrays, dram = {}, {}
    for name, a in layout(inputs).items():
        arrays[f"in_{name}"] = a
        dram[name] = nc.dram_tensor(f"in_{name}", a.shape, mybir.dt.from_np(a.dtype), kind="ExternalInput").ap()
    dram["out"] = nc.dram_tensor("out_features", [KT, P, T], F32, kind="ExternalOutput").ap()
    dram["bias_rows"] = nc.dram_tensor("bias_rows", [NM, P, BIAS_W], F32, kind="Internal").ap()
    build(nc, dram)
    r = run_bass_kernel_spmd(nc, [arrays], core_ids=[0])
    return np.ascontiguousarray(r.results[0]["out_features"].reshape(D, T).T)[None]
```

```python
from contextlib import ExitStack

import numpy as np

import concourse.bass as bass
from concourse import mybir

F32 = mybir.dt.float32
F32R = mybir.dt.float32r
ALU = mybir.AluOpType
ACT = mybir.ActivationFunctionType
AX = mybir.AxisListType

P = 128
T = 256
TT = T // P
D = 2048
KT = D // P
COLS = 512
CT = COLS // P
PAIR = COLS // 2
SLOT_K = 2
DFF = 8192
MLP_CHUNK = 1024
DFF2 = 5632
CONV_K = 31
GDN_K = 4
FFN_K = 3
HD = 128
NG = 8
NM = 8
NX = 4
CHUNK = 64
GW = NG * HD
NEG = -1e30
RAW = 4
SPLIT = 4
BUCKETS = 32
OUT_STEPS = 3
TURN_AFTER = 7



class Engine:

    def __init__(self, queue, sem):
        self.q, self.sem, self.count = queue, sem, 0

    def mark(self, instruction):
        self.count += 1
        instruction.then_inc(self.sem, 1)
        return (self.sem, self.count)

    def now(self):
        return (self.sem, self.count)

    def after(self, *marks):
        for m in marks:
            if isinstance(m, list):
                self.after(*m)
            elif m is not None:
                self.q.wait_ge(m[0], m[1])


class Ring:

    def __init__(self, buffers):
        self.buffers, self.free, self.at = buffers, [None] * len(buffers), -1
        self.held = [False] * len(buffers)

    def take(self):
        for n in range(1, len(self.buffers) + 1):
            i = (self.at + n) % len(self.buffers)
            if not self.held[i]:
                self.at, self.held[i] = i, True
                return i, self.buffers[i], self.free[i]
        raise AssertionError("every buffer of the ring is held")

    def give(self, i, *marks):
        self.free[i], self.held[i] = list(marks), False


def step(engine, waits, instruction):
    engine.after(*waits)
    return engine.mark(instruction(engine.q))


class Operand:

    def __init__(self, hi, lo):
        self.hi, self.lo = hi, lo



def rel_buckets(distance):
    max_exact = BUCKETS // 2
    nf = np.maximum(distance, 1).astype(np.float32)
    large = max_exact + (np.log(nf / np.float32(max_exact)) / np.float32(np.log(128 / max_exact))
                         * np.float32(BUCKETS - max_exact)).astype(np.int32)
    return np.where(distance < max_exact, distance, np.minimum(large, BUCKETS - 1))


MASKS = ["identity", "ones", "cumsum", "same_chunk", "causal_neg", "merge1"] + [f"merge{n}_t" for n in range(1, 7)]
BIAS_W = 384


def masks():
    i, j = np.arange(P)[:, None], np.arange(P)[None, :]
    same = (i // CHUNK) == (j // CHUNK)
    out = {
        "identity": i == j,
        "ones": np.ones((P, P), bool),
        "cumsum": same & (i <= j),
        "same_chunk": same,
    }
    out = {k: v.astype(np.float32) for k, v in out.items()}
    out["causal_neg"] = np.where(same & (i >= j), 0, NEG).astype(np.float32)
    for n in range(1, 7):
        m = ((i >> n) == (j >> n)) & (((i >> (n - 1)) & 1) == 1) & (((j >> (n - 1)) & 1) == 0)
        if n == 1:
            out["merge1"] = m.astype(np.float32)
        out[f"merge{n}_t"] = m.T.astype(np.float32)
    return np.stack([out[k] for k in MASKS], axis=1)


def bucket_rows():
    distance = 255 - np.arange(BIAS_W)
    hot = (rel_buckets(np.maximum(distance, 0))[None, :] == np.arange(BUCKETS)[:, None]).astype(np.float32)
    neg = np.where(distance >= 0, 0, NEG).astype(np.float32)
    return hot, np.broadcast_to(neg, (NM, BIAS_W)).copy()


VECTORS = [("norm1_g", 16), ("norm2_g", 16), ("cc_b_in", 32), ("cc_dw_b", 16), ("cc_ln_g", 16),
           ("cc_ln_b", 16), ("cc_b_out", 16), ("final_g", 16), ("mix_norm_g_2", 16), ("gdn_norm_g_2", 1),
           ("moba_norm_g_2", 1), ("xattn_norm_g_2", 16), ("mem_norm_g_2", 16), ("ffn_norm_g_2", 16),
           ("ffn_conv_b_2", 44), ("final_norm_g_2", 16)]
FILTERS = [("cc_dw", 16, CONV_K), ("gdn_conv_w_2", 24, GDN_K), ("ffn_conv_w_2", 44, FFN_K)]


def columns():
    at, n = {}, 0
    for name, tiles in VECTORS:
        at[name] = n
        n += tiles
    for name, tiles, taps in FILTERS:
        at[name] = n
        n += tiles * taps
    return at, n


COL, N_COLS = columns()



NORMS = ["norm1", "mem_norm", "layer_norm", "norm2", "final1", "mix_norm", "xattn_norm", "ffn_norm", "final2"]


class Program:
    def __init__(self, nc, stack, dram):
        self.nc, self.stack, self.dram = nc, stack, dram
        self.pe = Engine(nc.tensor, self.sem("pe_done"))
        self.dve = Engine(nc.vector, self.sem("dve_done"))
        self.act = Engine(nc.scalar, self.sem("act_done"))
        self.pool = Engine(nc.gpsimd, self.sem("pool_done"))
        self.sp = Engine(nc.sync, self.sem("sp_done"))
        self.dma_sems = {}
        self.done = {}
        self.pool_every = 1
        self.later = []

        self.x = self.sbuf("x_residual", [P, KT, T])
        self.h = Operand(self.sbuf("h_hi", [P, KT, T], F32R), self.sbuf("h_lo", [P, KT, T], F32R))
        self.mem_k = self.sbuf("mem_k", [P, NX, T])
        self.mem_v = self.sbuf("mem_v", [P, TT, NX * HD])
        self.w_raw = [self.sbuf(f"w_raw{i}", [P, SLOT_K, COLS]) for i in range(RAW)]
        self.w_hi = [self.sbuf(f"w_hi{i}", [P, SLOT_K, COLS], F32R) for i in range(SPLIT)]
        self.w_lo = [self.sbuf(f"w_lo{i}", [P, SLOT_K, COLS], F32R) for i in range(SPLIT)]
        self.scratch = Ring([self.sbuf(f"scratch{i}", [P, CT, T]) for i in range(3)])
        self.sum_sq = self.sbuf("sum_sq", [P, 2, T])
        self.partial = self.sbuf("partial_sum", [P, T])
        rows = self.sbuf("rows", [P, 2, T])
        self.row = {norm: rows[:, i % 2, :] for i, norm in enumerate(NORMS)}
        self.double_gain = self.sbuf("double_gain", [P, KT])
        self.mask = self.sbuf("masks", [P, len(MASKS), P])
        self.cols = self.sbuf("feature_columns", [P, N_COLS])
        self.eps = self.sbuf("epsilons", [P, 3])
        self.acc = Ring([self.psum(f"product{i}", [P, 2 * 512]) for i in range(2)])
        self.bank = Ring([self.psum(f"small{i}", [P, 512]) for i in range(4)])

    def sbuf(self, name, shape, dt=F32, stack=None):
        return (stack or self.stack).enter_context(self.nc.sbuf_tensor(name, shape, dt))[:]

    def psum(self, name, shape):
        return self.stack.enter_context(self.nc.psum_tensor(name, shape, F32))[:]

    def sem(self, name):
        return self.stack.enter_context(self.nc.semaphore(name))

    def col(self, name, i, n=1):
        return self.cols[:, COL[name] + i:COL[name] + i + n]

    def m(self, name):
        return self.mask[:, MASKS.index(name), :]

    def dma(self, engine, out, in_, name):
        if name not in self.dma_sems:
            self.dma_sems[name] = [self.sem(name), 0]
        s = self.dma_sems[name]
        s[1] += 16
        engine.q.dma_start(out, in_).then_inc(s[0], 16)
        return (s[0], s[1])

    def phase(self):
        for e in (self.dve, self.act, self.pool):
            e.after(*[o.now() for o in (self.pe, self.dve, self.act, self.pool)])

    def plan_weights(self):
        d, plan = self.dram, []

        def block(name, col, k0=0, k=D):
            for r in range(k0, k0 + k, SLOT_K * P):
                w = d[name][r:r + SLOT_K * P, col:col + COLS]
                plan.append(((name, r, col), [w.rearrange("(k p) n -> p k n", p=P)]))

        for b in range(D // PAIR):
            for r in range(0, D, SLOT_K * P):
                w = d["cc_w_in"][r:r + SLOT_K * P, :].rearrange("(k p) n -> p k n", p=P)
                plan.append((("cc_w_in", r, b), [w[:, :, D + b * PAIR:D + (b + 1) * PAIR], w[:, :, b * PAIR:(b + 1) * PAIR]]))
        for b in range(2):
            block("w_xkv_2", b * COLS)
        for b in range(CT):
            block("cc_w_out", b * COLS)
        for kind, c in mlp_order():
            if kind == "up":
                for b in range(MLP_CHUNK // COLS):
                    block("mlp_w1", c * MLP_CHUNK + b * COLS)
            else:
                for b in range(CT):
                    block("mlp_w2", b * COLS, c * MLP_CHUNK, MLP_CHUNK)
        for g in range(2):
            for part in range(4):
                block("w_in_2", part * GW + g * COLS)
        for b in MOBA_BLOCKS:
            block("w_in_2", 4 * GW + 2 * NG + b * COLS)
        for half, b in w_out_order():
            block("w_out_2", b * COLS, half * GW, GW)
        block("w_xq_2", 0)
        for b in range(CT):
            block("w_xo_2", b * COLS, 0, NX * HD)
        for kind, c in ffn_order():
            if kind == "up":
                block("w_gate_2", c * COLS)
                block("w_up_2", c * COLS)
            else:
                for b in range(CT):
                    block("w_down_2", b * COLS, c * COLS, COLS)
        self.plan = plan
        n = len(plan)
        self.n_loaded = self.n_split = self.n_used = 0
        self.slot_landed = [None] * n
        self.slot_split = [None] * n
        self.slot_used = [None] * n

    def load_slot(self):
        i = self.n_loaded
        if i >= len(self.plan):
            return
        self.n_loaded += 1
        if i >= RAW:
            self.sp.after(self.slot_split[i - RAW])
        parts = self.plan[i][1]
        width = COLS // len(parts)
        for n, part in enumerate(parts):
            self.slot_landed[i] = self.dma(self.sp, self.w_raw[i % RAW][:, :, n * width:(n + 1) * width], part,
                                           f"w_landed{i % RAW}")

    def split_slot(self):
        i = self.n_split
        if i >= len(self.plan):
            return
        self.n_split += 1
        raw, hi, lo = self.w_raw[i % RAW], self.w_hi[i % SPLIT], self.w_lo[i % SPLIT]
        used = self.slot_used[i - SPLIT] if i >= SPLIT else None
        self.act.after(self.slot_landed[i], used)
        hi_done = self.act.mark(self.act.q.activation(hi, raw, ACT.Copy))
        e = self.pool if self.on_pool(i) else self.dve
        e.after(hi_done)
        lo_done = e.mark(e.q.tensor_tensor(lo, raw, hi.bitcast(F32), ALU.subtract))
        self.slot_split[i] = lo_done
        self.load_slot()

    def on_pool(self, i):
        return self.pool_every and i % self.pool_every == 0

    def use_slot(self, name, row, col):
        i = self.n_used
        assert self.plan[i][0] == (name, row, col), (self.plan[i][0], (name, row, col))
        self.n_used += 1
        self.pe.after(self.slot_split[i])
        return i, self.w_hi[i % SPLIT], self.w_lo[i % SPLIT]

    def slot_done(self, i, mark):
        self.slot_used[i] = mark
        self.split_slot()
        if self.later:
            self.later[0][0] -= 1
            if self.later[0][0] <= 0:
                self.later.pop(0)[1]()

    def put_off(self, task, slots=1):
        self.later.append([slots, task])

    def do_later(self):
        while self.later:
            self.later.pop(0)[1]()

    def product(self, name, col, x, split, evict, row=0, k_tiles=None, tokens_out=False, part_of=None):
        k_tiles = range(x.hi.shape[1]) if k_tiles is None else k_tiles
        held, opening, closing = part_of or ({}, True, True)
        if opening:
            held["slot"], held["psum"], free = self.acc.take()
            self.pe.after(free)
        slot, psum = held["slot"], held["psum"]
        q = self.pe.q
        for s in range(len(k_tiles) // SLOT_K):
            i, hi, lo = self.use_slot(name, row + s * SLOT_K * P, col)
            last = None
            parts = range(TT) if tokens_out else range(CT)
            for part in parts:
                for kk in range(SLOT_K):
                    n_k = s * SLOT_K + kk
                    kt = k_tiles[n_k]
                    if part == 0 and kt % CT == 0:
                        self.pe.after(self.done[split, kt])
                    if tokens_out:
                        out = psum[:, part * COLS:(part + 1) * COLS]
                        t = slice(part * P, (part + 1) * P)
                        triples = [(x.hi[:, kt, t], hi[:, kk, :]), (x.lo[:, kt, t], hi[:, kk, :]),
                                   (x.hi[:, kt, t], lo[:, kk, :])]
                        opens = True
                    else:
                        out = psum[:, part * T:(part + 1) * T]
                        n = slice(part * P, (part + 1) * P)
                        triples = [(hi[:, kk, n], x.hi[:, kt, :]), (hi[:, kk, n], x.lo[:, kt, :]),
                                   (lo[:, kk, n], x.hi[:, kt, :])]
                        opens = part % 2 == 0
                    for j, (stationary, moving) in enumerate(triples):
                        first = opening and n_k == 0 and j == 0
                        final = closing and n_k == len(k_tiles) - 1 and j == 2
                        last = q.matmul(out, stationary, moving, start=first and opens, stop=final,
                                        skip_group_check=True)
            mark = self.pe.mark(last)
            self.done[name] = mark
            if closing and s == len(k_tiles) // SLOT_K - 1:
                self.acc.give(slot, evict(psum, mark))
            self.slot_done(i, mark)
            yield

    def split_into(self, src, made, x, first, n, name, target_free):
        hi, lo = x.hi[:, first:first + n, :], x.lo[:, first:first + n, :]
        self.act.after(made, target_free)
        hi_done = self.act.mark(self.act.q.activation(hi, src, ACT.Copy))
        self.dve.after(hi_done)
        lo_done = self.dve.mark(self.dve.q.tensor_tensor(lo, src, hi.bitcast(F32), ALU.subtract))
        for i in range(first, first + n):
            self.done[name, i] = lo_done
        return lo_done

    def add_squares(self, src, made, g, which=0, gain=None):
        act, dve = self.act, self.dve
        i, sq, free = self.scratch.take()
        act.after(made, free)
        if gain is None:
            done = act.mark(act.q.activation(sq, src, ACT.Square))
        else:
            for t in range(CT):
                done = act.mark(act.q.activation(sq[:, t, :], src[:, t, :], ACT.Square, scale=self.col(gain, g * CT + t)))
        tiles = sq.rearrange("p k t -> p t k")
        out = self.sum_sq[:, which, :]
        if g == 0:
            r = step(dve, [done, self.done.get("total")], lambda q: q.tensor_reduce(out, tiles, AX.X, ALU.add))
            self.done["sums"] = r
        else:
            r = step(dve, [done, self.done["sums"]], lambda q: q.tensor_reduce(self.partial, tiles, AX.X, ALU.add))
            self.done["sums"] = step(dve, [r], lambda q: q.tensor_tensor(out, out, self.partial, ALU.add))
        self.scratch.give(i, r)
        return done

    def total(self, n=1):
        self.do_later()
        i, bank, free = self.bank.take()
        out = bank[:, 0:n * T]
        done = step(self.pe, [self.done["sums"], free], lambda q: q.matmul(
            out, self.m("ones"), self.sum_sq[:, 0:n, :].rearrange("p n t -> p (n t)"), start=True, stop=True))
        self.done["total"] = done
        return i, out, done

    def inverse_root(self, psum, marks, out, scale, eps):
        root = step(self.act, [marks], lambda q: q.activation(out, psum, ACT.Sqrt, bias=self.eps[:, eps:eps + 1], scale=scale))
        return root, step(self.dve, [root], lambda q: q.reciprocal(out, out))

    def rms_row(self, norm, row_free):
        i, psum, done = self.total()
        root, self.done[norm, "row"] = self.inverse_root(psum, [done, row_free], self.row[norm], 1.0 / D, 0)
        self.bank.give(i, root)

    def times_row(self, norm, out, psum, marks):
        n = out.shape[1]
        row = self.row[norm].unsqueeze(1).broadcast_to([P, n, T])
        src = psum.rearrange("p (k t) -> p k t", t=T)
        done = step(self.dve, [marks, self.done[norm, "row"]], lambda q: q.tensor_tensor(out, src, row, ALU.mult))
        self.done[norm, "applied"] = done
        return done

    def norm_group(self, norm, src, made, gain, g, out, out_free):
        self.dve.after(made, self.done[norm, "row"], out_free)
        for t in range(CT):
            done = self.dve.mark(self.dve.q.scalar_tensor_tensor(
                out=out[:, t, :], in0=src[:, t, :], scalar=self.col(gain, g * CT + t),
                in1=self.row[norm], op0=ALU.mult, op1=ALU.mult))
        self.done[norm, "applied"] = self.done[norm, "group", g] = done
        return done

    def norm_to_operand(self, norm, src, made, gain, x):
        self.rms_row(norm, None)
        yield
        for g in range(CT):
            i, tmp, free = self.scratch.take()
            done = self.norm_group(norm, src[:, g * CT:(g + 1) * CT, :], made[g], gain, g, tmp, free)
            self.scratch.give(i, self.split_into(tmp, done, x, g * CT, CT, norm, None))
            yield

    def prepare(self, norm, g, gain, x, added, target_free):
        i, tmp, free = self.scratch.take()
        src = self.x[:, g * CT:(g + 1) * CT, :]
        self.dve.after(added, free)
        for t in range(CT):
            done = self.dve.mark(self.dve.q.tensor_scalar(tmp[:, t, :], src[:, t, :], gain(g * CT + t), None, ALU.mult))
        self.done[norm, "scaled", g] = done
        self.scratch.give(i, self.split_into(tmp, done, x, g * CT, CT, norm, target_free))

    def residual(self, stage, b, before, bias=None, after=None):
        def evict(psum, mark):
            x = self.x[:, b * CT:(b + 1) * CT, :]
            self.dve.after(mark, [self.done[name] for name in before])
            y = psum.rearrange("p (k t) -> p k t", t=T)
            if bias is None:
                done = self.dve.mark(self.dve.q.tensor_tensor(x, x, y, ALU.add))
            else:
                for t in range(CT):
                    done = self.dve.mark(self.dve.q.scalar_tensor_tensor(
                        out=x[:, t, :], in0=y[:, t, :], scalar=self.col(bias, b * CT + t), in1=x[:, t, :],
                        op0=ALU.add, op1=ALU.add))
            self.done[stage, b] = done
            if after is not None:
                after(b, done)
            return done
        return evict

    def next_operand(self, norm, gain, x, target_free, second_gain=None):
        def after(b, added):
            group = self.x[:, b * CT:(b + 1) * CT, :]
            if x is not None:
                self.prepare(norm, b, gain, x, added, self.done[target_free] if target_free else None)

            def squares():
                self.done[norm, "squares", b] = self.add_squares(group, added, b)

            def second_squares():
                self.done[norm, "second squares", b] = self.add_squares(group, added, b, which=1, gain=second_gain)
            self.put_off(squares)
            if second_gain is not None:
                self.put_off(second_squares)
        return after

    def gain(self, name):
        return lambda k: self.col(name, k)

    def constants(self):
        d = self.dram
        self.pe.after(self.dma(self.act, self.mask, d["masks"], "masks_landed"))
        landed = self.dma(self.act, self.cols, d["feature_columns"], "columns_landed")
        self.dve.after(landed, (self.dma_sems["masks_landed"][0], 16))
        self.act.after(landed, (self.dma_sems["masks_landed"][0], 16))
        self.pool.after(landed, (self.dma_sems["masks_landed"][0], 16))
        for i, v in enumerate([1e-6, 1e-5, 128e-6]):
            done = self.pool.mark(self.pool.q.memset(self.eps[:, i:i + 1], v))
        self.act.after(done)
        self.done["double_gain"] = step(self.dve, [], lambda q: q.tensor_tensor(
            self.double_gain, self.col("final_g", 0, KT), self.col("mix_norm_g_2", 0, KT), ALU.mult))


MOBA_BLOCKS = [0, 2, 4, 1, 3, 5]


def w_out_order():
    return [(0, 0), (0, 1), (1, 0), (1, 1), (0, 2), (1, 2), (0, 3), (1, 3)]


def mlp_order():
    n = DFF // MLP_CHUNK
    out = [("up", 0)]
    for c in range(1, n):
        out += [("up", c), ("down", c - 1)]
    return out + [("down", n - 1)]


def ffn_order():
    n = DFF2 // COLS
    out = [("up", 0)]
    for c in range(1, n):
        out += [("up", c), ("down", c - 1)]
    return out + [("down", n - 1)]


def with_row(product, make_row, slot=3):
    for n, _ in enumerate(product):
        if n == slot:
            make_row()
        yield


def run(*steps):
    for s in steps:
        for _ in s:
            pass



def conformer(p):
    d, dve, act, pe, pool = p.dram, p.dve, p.act, p.pe, p.pool
    stack = p.phase_stack
    mem = Operand(p.sbuf("mem_hi", [P, KT, T], F32R, stack), p.sbuf("mem_lo", [P, KT, T], F32R, stack))
    p.mid = mem
    u = p.sbuf("conv_out", [P, KT, T], stack=stack)
    mem_x = u
    pt = PAIR // P
    gate = Ring([p.sbuf(f"gate{i}", [P, pt, T], stack=stack) for i in range(2)])
    glu = Ring([p.sbuf(f"glu{i}", [P, pt, CONV_K - 1 + T], stack=stack) for i in range(3)])
    mean = p.sbuf("mean", [P, T], stack=stack)

    for g in range(CT):
        tiles = slice(g * CT, (g + 1) * CT)
        p.done["x_landed", g] = p.dma(p.sp, p.x[:, tiles, :], d["x"][tiles].rearrange("k p t -> p k t"), f"x_landed{g}")
    for _ in range(RAW):
        p.load_slot()
    p.constants()
    bias_rows(p)
    mem_ready = []
    for g in range(CT):
        tiles = slice(g * CT, (g + 1) * CT)
        mem_ready.append(p.dma(p.act, mem_x[:, tiles, :], d["mem"][tiles].rearrange("k p t -> p k t"), f"mem_landed{g}"))
    for i, buf in enumerate(glu.buffers):
        glu.give(i, step(pool, [], lambda q: q.memset(buf[:, :, 0:CONV_K - 1], 0.0)))

    for g in range(CT):
        tiles = slice(g * CT, (g + 1) * CT)
        p.done["norm1", "squares", g] = p.add_squares(p.x[:, tiles, :], p.done["x_landed", g], g)
    for _ in range(SPLIT):
        p.split_slot()
    run(p.norm_to_operand("norm1", p.x, [p.done["x_landed", g] for g in range(CT)], "norm1_g", p.h))

    def norm_mem():
        for g in range(CT):
            p.add_squares(mem_x[:, g * CT:(g + 1) * CT, :], mem_ready[g], g)
            if g % 2:
                yield
        yield from p.norm_to_operand("mem_norm", mem_x, mem_ready, "mem_norm_g_2", mem)

    units, u_ready = [], [None] * KT

    def evict_pair(b):
        def evict(psum, mark):
            gi, g, free = gate.take()
            act.after(mark, free)
            for t in range(pt):
                g_done = act.mark(act.q.activation(g[:, t, :], psum[:, t * T:(t + 1) * T], ACT.Sigmoid,
                                                   bias=p.col("cc_b_in", KT + b * pt + t)))
            i, out, free = glu.take()
            dve.after(mark, g_done, free)
            for t in range(pt):
                done = dve.mark(dve.q.scalar_tensor_tensor(
                    out=out[:, t, CONV_K - 1:], in0=psum[:, (pt + t) * T:(pt + t + 1) * T],
                    scalar=p.col("cc_b_in", b * pt + t), in1=g[:, t, :], op0=ALU.add, op1=ALU.mult))
            gate.give(gi, done)
            units.append((b, i, out, done))
            return [g_done, done]
        return evict

    def convolve():
        while len(units) or not products_done:
            if not units:
                yield
                continue
            b, i, src, mark = units.pop(0)
            dve.after(mark, p.done["mem_norm", "group", b * pt // CT])
            done = [None] * pt
            for j in range(CONV_K):
                for t in range(pt):
                    k = b * pt + t
                    out, tap = u[:, k, :], src[:, t, j:j + T]
                    w = p.col("cc_dw", k * CONV_K + j)
                    dve.after(done[t])
                    if j == 0:
                        ins = dve.q.tensor_scalar(out, tap, w, p.col("cc_dw_b", k), ALU.mult, ALU.add)
                    else:
                        ins = dve.q.scalar_tensor_tensor(out=out, in0=tap, scalar=w, in1=out, op0=ALU.mult, op1=ALU.add)
                    done[t] = dve.mark(ins)
                if j % 3 == 2:
                    yield
            glu.give(i, done)
            for t in range(pt):
                u_ready[b * pt + t] = done[t]

    def keys(psum, mark):
        p.mem_k_ready = step(act, [mark], lambda q: q.activation(
            p.mem_k, psum.rearrange("p (k t) -> p k t", t=T), ACT.Copy))
        return p.mem_k_ready

    def values(psum, mark):
        p.mem_v_ready = step(act, [mark], lambda q: q.activation(
            p.mem_v, psum.rearrange("p (k n) -> p k n", n=COLS), ACT.Copy))
        return p.mem_v_ready

    def products():
        for b in range(D // PAIR):
            yield from p.product("cc_w_in", b, p.h, "norm1", evict_pair(b))
        yield from p.product("w_xkv_2", 0, mem, "mem_norm", keys)
        yield from p.product("w_xkv_2", COLS, mem, "mem_norm", values, tokens_out=True)

    products_done = False
    side, conv = norm_mem(), convolve()
    for _ in products():
        next(side, None)
        next(conv, None)
    products_done = True
    p.pool_every = 0
    run(side, conv)

    i, bank, free = p.bank.take()
    pe.after(free)
    for k in range(KT):
        pe.after(u_ready[k])
        ins = pe.q.matmul(bank[:, 0:T], p.m("ones"), u[:, k, :], start=k == 0, stop=k == KT - 1)
    summed = pe.mark(ins)
    mean_ready = step(act, [summed], lambda q: q.activation(mean, bank[:, 0:T], ACT.Copy, scale=1.0 / D))
    p.bank.give(i, mean_ready)
    i, bank, free = p.bank.take()
    pe.after(free)
    centred = [None] * CT
    for g in range(CT):
        ug = u[:, g * CT:(g + 1) * CT, :]
        centred[g] = step(dve, [mean_ready], lambda q: q.tensor_tensor(
            ug, ug, mean.unsqueeze(1).broadcast_to([P, CT, T]), ALU.subtract))
        si, sq, sfree = p.scratch.take()
        squared = step(act, [centred[g], sfree], lambda q: q.activation(sq, ug, ACT.Square))
        pe.after(squared)
        for t in range(CT):
            ins = pe.q.matmul(bank[:, 0:T], p.m("ones"), sq[:, t, :], start=g == 0 and t == 0, stop=g == CT - 1 and t == CT - 1)
        summed = pe.mark(ins)
        p.scratch.give(si, summed)
    row = p.row["layer_norm"]
    root, ready = p.inverse_root(bank[:, 0:T], [summed, p.done["norm1", "applied"]], row, 1.0 / D, 1)
    p.bank.give(i, root)
    for g in range(CT):
        ug = u[:, g * CT:(g + 1) * CT, :]
        done = step(dve, [ready], lambda q: q.tensor_tensor(
            ug, ug, row.unsqueeze(1).broadcast_to([P, CT, T]), ALU.mult))
        p.done["layer_norm", "applied"] = done
        i, tmp, free = p.scratch.take()
        act.after(done, free)
        for t in range(CT):
            k = g * CT + t
            s = act.mark(act.q.activation(tmp[:, t, :], u[:, k, :], ACT.Silu, scale=p.col("cc_ln_g", k),
                                          bias=p.col("cc_ln_b", k)))
        p.scratch.give(i, p.split_into(tmp, s, mem, g * CT, CT, "conv_out", p.done["w_xkv_2"]))
    after = p.next_operand("norm2", p.gain("norm2_g"), p.h, "cc_w_in")
    for b in range(CT):
        before = [("x_landed", b), ("norm1", "squares", b), ("norm1", "group", b)]
        run(p.product("cc_w_out", b * COLS, mem, "conv_out", p.residual("conformer", b, before, "cc_b_out", after)))


def mlp(p):
    act = p.act
    ct = MLP_CHUNK // P
    mids = [Operand(p.mid.hi[:, i * ct:(i + 1) * ct, :], p.mid.lo[:, i * ct:(i + 1) * ct, :]) for i in range(2)]
    last = DFF // MLP_CHUNK - 1
    after = p.next_operand("mix_norm", lambda k: p.double_gain[:, k:k + 1], p.h, "mlp_w1", "final_g")

    def squared_relu(c, mid, first):
        def evict(psum, mark):
            i, r, free = p.scratch.take()
            done = scaled = p.times_row("norm2", r, psum, [mark, free])
            for f in (ACT.Relu, ACT.Square):
                done = step(act, [done], lambda q: q.activation(r, r, f))
            used = p.done["mlp_w2"] if c >= 2 else p.done["cc_w_out"]
            p.scratch.give(i, p.split_into(r, done, mid, first, CT, ("hidden", c), used))
            return scaled
        return evict

    for kind, c in mlp_order():
        mid = mids[c % 2]
        if kind == "up":
            for b in range(MLP_CHUNK // COLS):
                up = p.product("mlp_w1", c * MLP_CHUNK + b * COLS, p.h, "norm2", squared_relu(c, mid, b * CT))
                if c == 0 and b == 0:
                    up = with_row(up, lambda: p.rms_row("norm2", p.done["mem_norm", "applied"]))
                run(up)
        else:
            for b in range(CT):
                before = [(("mlp", c - 1), b)] if c else [("conformer", b), ("norm2", "scaled", b), ("norm2", "squares", b)]
                add = p.residual(("mlp", c), b, before, after=after if c == last else None)
                run(p.product("mlp_w2", b * COLS, mid, ("hidden", c), add, row=c * MLP_CHUNK))


def two_norms(p):
    i, psum, done = p.total(2)
    r1, r2 = p.row["final1"], p.row["mix_norm"]
    _, r1_ready = p.inverse_root(psum[:, 0:T], [done, p.done["layer_norm", "applied"]], r1, 1.0 / D, 0)
    p.done["final1", "row"] = r1_ready
    m = step(p.dve, [r1_ready, p.done["norm2", "applied"]],
             lambda q: q.tensor_tensor(r2, psum[:, T:2 * T], r1, ALU.mult))
    p.bank.give(i, m)
    m = step(p.dve, [m], lambda q: q.tensor_tensor(r2, r2, r1, ALU.mult))
    _, m = p.inverse_root(r2, [m], r2, 1.0 / D, 0)
    p.done["mix_norm", "row"] = step(p.dve, [m], lambda q: q.tensor_tensor(r2, r2, r1, ALU.mult))
    last = DFF // MLP_CHUNK - 1

    def scale(g):
        xg = p.x[:, g * CT:(g + 1) * CT, :]
        p.norm_group("final1", xg, p.done[("mlp", last), g], "final_g", g, xg,
                     [p.done["mix_norm", "squares", g], p.done["mix_norm", "second squares", g],
                      p.done["mix_norm", "scaled", g]])
    for g in range(CT):
        p.put_off(lambda g=g: scale(g))


def last_norm(p):
    p.rms_row("final2", p.done["xattn_norm", "applied"])
    last = DFF2 // COLS - 1
    for g in range(CT):
        xg = p.x[:, g * CT:(g + 1) * CT, :]
        p.norm_group("final2", xg, p.done[("ffn", last), g], "final_norm_g_2", g, xg, p.done["final2", "squares", g])


def store_x(p):
    for g in range(CT):
        tiles = slice(g * CT, (g + 1) * CT)
        p.sp.after(p.done["final2", "group", g])
        stored = p.dma(p.sp, p.dram["out"][tiles].rearrange("k p t -> p k t"), p.x[:, tiles, :], "x_stored")
    p.sp.after(stored, p.bias_rows_stored)



def bias_rows(p):
    d, s = p.dram, p.phase_stack
    hot = p.sbuf("bucket_one_hot", [BUCKETS, BIAS_W], stack=s)
    neg = p.sbuf("bucket_neg", [NM, BIAS_W], stack=s)
    table = p.sbuf("rel_bias", [BUCKETS, NM], stack=s)
    landed = [p.dma(p.act, hot, d["bucket_one_hot"], "one_hot_landed"),
              p.dma(p.act, neg, d["bucket_neg"], "bias_neg_landed"),
              p.dma(p.act, table, d["rel_bias"], "rel_bias_landed")]
    i, bank, free = p.bank.take()
    rows = step(p.pe, [landed, free], lambda q: q.matmul(bank[0:NM, 0:BIAS_W], table, hot, start=True, stop=True))
    done = step(p.dve, [rows, landed], lambda q: q.tensor_tensor(neg, neg, bank[0:NM, 0:BIAS_W], ALU.add))
    p.bank.give(i, done)
    p.act.after(done)
    p.bias_rows_stored = p.dma(p.act, d["bias_rows"], neg.unsqueeze(1).broadcast_to([NM, P, BIAS_W]), "bias_rows_stored")


def gates(p, s):
    d, dve, act, pe = p.dram, p.dve, p.act, p.pe
    w, w_hi, w_lo = s.w_ba, s.w_ba_hi, s.w_ba_lo
    yield
    yield
    hi_done = step(act, [s.w_ba_landed], lambda q: q.activation(w_hi, w, ACT.Copy))
    lo_done = step(dve, [hi_done], lambda q: q.tensor_tensor(w_lo, w, w_hi.bitcast(F32), ALU.subtract))
    yield
    token_column(p, s)
    yield
    yield
    i, bank, free = p.bank.take()
    pe.after(free, hi_done, lo_done, [p.done["mix_norm", k] for k in range(0, KT, CT)])
    n = 2 * NG
    for t in range(TT):
        tok = slice(t * P, (t + 1) * P)
        for k in range(KT):
            for j, (x, y) in enumerate([(p.h.hi, w_hi), (p.h.lo, w_hi), (p.h.hi, w_lo)]):
                ins = pe.q.matmul(bank[:, t * n:(t + 1) * n], x[:, k, tok], y[:, k, :],
                                  start=k == 0 and j == 0, stop=k == KT - 1 and j == 2)
    made = pe.mark(ins)
    sm = s.small
    e, ab, sp = sm[:, 0], sm[:, 1], sm[:, 2]
    for t in range(TT):
        made = step(act, [made, s.token_ready], lambda q: q.activation(
            s.ba[:, t, :], bank[:, t * n:(t + 1) * n], ACT.Copy, scale=s.token_col[:, t:t + 1]))
    p.bank.give(i, made)
    b_in, a_in = s.ba[:, :, 0:NG], s.ba[:, :, NG:n]
    read_b = m1 = step(act, [made], lambda q: q.activation(s.beta, b_in, ACT.Exp, scale=-1.0))
    m1 = step(dve, [m1], lambda q: q.tensor_scalar(s.beta, s.beta, 1.0, None, ALU.add))
    beta = step(dve, [m1], lambda q: q.reciprocal(s.beta, s.beta))
    m2 = step(dve, [read_b, s.heads_landed], lambda q: q.tensor_tensor(
        e, a_in, s.dt_bias.unsqueeze(1).broadcast_to([P, TT, NG]), ALU.add))
    m3 = step(act, [m2], lambda q: q.activation(ab, e, ACT.Abs))
    m4 = step(act, [m3], lambda q: q.activation(ab, ab, ACT.Exp, scale=-1.0))
    m4 = step(act, [m4], lambda q: q.activation(ab, ab, ACT.Ln, bias=p.m("ones")[:, 0:1]))
    m5 = step(dve, [m4], lambda q: q.scalar_tensor_tensor(out=sp, in0=e, scalar=0.0, in1=ab, op0=ALU.max, op1=ALU.add))
    m6 = step(act, [s.heads_landed], lambda q: q.activation(s.a_log, s.a_log, ACT.Exp))
    g_done = step(dve, [m5, m6], lambda q: q.scalar_tensor_tensor(
        out=s.g, in0=sp, scalar=-1.0, in1=s.a_log.unsqueeze(1).broadcast_to([P, TT, NG]), op0=ALU.mult, op1=ALU.mult))
    yield
    yield
    i, bank, free = p.bank.take()
    pe.after(g_done, free)
    for t in range(TT):
        pe.q.matmul(bank[:, t * NG:(t + 1) * NG], p.m("cumsum"), s.g[:, t, :], start=True, stop=True)
        ins = pe.q.matmul(bank[:, (TT + t) * NG:(TT + t + 1) * NG], p.m("same_chunk"), s.g[:, t, :], start=True, stop=True)
    sums = pe.mark(ins)
    upto = bank[:, 0:TT * NG].rearrange("p (t n) -> p t n", t=TT)
    whole = bank[:, TT * NG:2 * TT * NG].rearrange("p (t n) -> p t n", t=TT)
    c1 = step(dve, [sums], lambda q: q.tensor_copy(s.cum, upto))
    c2 = step(dve, [c1], lambda q: q.tensor_tensor(s.k_decay, whole, s.cum, ALU.subtract))
    c3 = step(act, [c2], lambda q: q.activation(s.k_decay, s.k_decay, ACT.Exp))
    c4 = step(act, [c1], lambda q: q.activation(s.beta_decay, s.cum, ACT.Exp))
    p.bank.give(i, c1, c2)
    c5 = step(dve, [c4, beta], lambda q: q.tensor_tensor(s.beta_decay, s.beta_decay, s.beta, ALU.mult))
    s.gates_ready = [beta, g_done, c1, c3, c5]


def conv_silu(p, s, g, part, out, free):
    dve, act = p.dve, p.act

    def evict(psum, mark):
        i, pad, pad_free = s.pad.take()
        copied = p.times_row("mix_norm", pad[:, :, GDN_K - 1:], psum, [mark, pad_free])
        done = [None] * CT

        def taps(j):
            if j == 0:
                dve.after(copied, free)
            for t in range(CT):
                w = p.col("gdn_conv_w_2", (part * NG + g * CT + t) * GDN_K + j)
                tap = pad[:, t, j:j + T]
                if j == 0:
                    done[t] = dve.mark(dve.q.tensor_scalar(out[:, t, :], tap, w, None, ALU.mult))
                else:
                    done[t] = step(dve, [done[t]], lambda q: q.scalar_tensor_tensor(
                        out=out[:, t, :], in0=tap, scalar=w, in1=out[:, t, :], op0=ALU.mult, op1=ALU.add))
            if j == GDN_K - 1:
                s.pad.give(i, done[-1])

        def silu():
            s.conv_ready[g, part] = step(act, [done[-1]], lambda q: q.activation(out, out, ACT.Silu))
        for j in range(GDN_K):
            p.put_off(lambda j=j: taps(j))
        p.put_off(silu)
        return copied
    return evict


def l2_normalise(p, x, ready, scale, eps):
    i, sq, free = p.scratch.take()
    squared = step(p.act, [ready, free], lambda q: q.activation(sq, x, ACT.Square))
    flat = sq.rearrange("p k t -> p (k t)")
    done = None
    yield None
    yield None
    for half in range(2):
        cols = slice(half * 512, (half + 1) * 512)
        bi, bank, bfree = p.bank.take()
        summed = step(p.pe, [squared, bfree], lambda q: q.matmul(bank, p.m("ones"), flat[:, cols], start=True, stop=True))
        root = step(p.act, [summed], lambda q: q.activation(flat[:, cols], bank, ACT.Sqrt, bias=p.eps[:, eps:eps + 1], scale=scale))
        p.bank.give(bi, root)
        inv = step(p.dve, [root], lambda q: q.reciprocal(flat[:, cols], flat[:, cols]))
        xs = x.rearrange("p k t -> p (k t)")[:, cols]
        done = step(p.dve, [inv], lambda q: q.tensor_tensor(xs, xs, flat[:, cols], ALU.mult))
        yield None
    p.scratch.give(i, done)
    yield done


def head_norm(p, o, ready, gain, gate=None, gate_ready=None):
    i, sq, free = p.scratch.take()
    squared = step(p.act, [ready, free], lambda q: q.activation(sq, o, ACT.Square))
    yield None
    flat, of = sq.rearrange("p k t -> p (k t)"), o.rearrange("p k t -> p (k t)")
    for half in range(2):
        cols = slice(half * 512, (half + 1) * 512)
        bi, bank, bfree = p.bank.take()
        summed = step(p.pe, [squared, bfree], lambda q: q.matmul(bank, p.m("ones"), flat[:, cols], start=True, stop=True))
        root = step(p.act, [summed], lambda q: q.activation(flat[:, cols], bank, ACT.Sqrt, bias=p.eps[:, 0:1], scale=1.0 / HD))
        p.bank.give(bi, root)
        inv = step(p.dve, [root], lambda q: q.reciprocal(flat[:, cols], flat[:, cols]))
        done = step(p.dve, [inv], lambda q: q.scalar_tensor_tensor(
            out=of[:, cols], in0=of[:, cols], scalar=p.col(gain, 0), in1=flat[:, cols], op0=ALU.mult, op1=ALU.mult))
        if gate is not None:
            gf = gate.rearrange("p k t -> p (k t)")[:, cols]
            done = step(p.dve, [done, gate_ready], lambda q: q.tensor_tensor(of[:, cols], of[:, cols], gf, ALU.mult))
        yield None
    p.scratch.give(i, done)
    yield done


def transposes(p, dst_bank, blocks):
    for n, b in enumerate(blocks):
        ins = p.pe.q.transpose(dst_bank[:, n * P:(n + 1) * P], b, p.m("identity"))
    return p.pe.mark(ins)


def delta_rule(p, s, g):
    pe, dve, act, pool = p.pe, p.dve, p.act, p.pool
    qt, kt, vb, z = s.q_t[g], s.k_t[g], s.v_beta[g], s.z[g]
    heads = range(CT)
    hs = slice(g * CT, (g + 1) * CT)
    four = lambda ap: ap.unsqueeze(1).broadcast_to([P, CT, P])
    bank4 = lambda b: b.rearrange("p (h n) -> p h n", h=CT)

    work_free = s.chunks_done[0] if g else None

    def row(t):
        return slice(t * P, (t + 1) * P)

    gi, spread_g, gfree = p.scratch.take()
    dve.after(s.gates_ready, gfree)
    for t in range(TT):
        spread = dve.mark(dve.q.tensor_copy(spread_g[:, :, row(t)], s.g[:, t, hs].unsqueeze(2).broadcast_to([P, CT, P])))

    q_ready = k_ready = None
    for q_ready in l2_normalise(p, qt, s.conv_ready[g, 0], float(HD), 2):
        yield

    decay_ready, (eg_i, eg, eg_free) = [None] * TT, p.scratch.take()
    for t in range(TT):
        bi, bank, bfree = p.bank.take()
        pe.after(spread, bfree)
        for h in heads:
            ins = pe.q.matmul(bank[:, row(h)], spread_g[:, h, row(t)], p.m("cumsum"), start=True, stop=True)
        rows = pe.mark(ins)
        if t == TT - 1:
            p.scratch.give(gi, rows)
        d = s.decay[t]
        grown = step(act, [rows, eg_free], lambda q: q.activation(eg[:, :, row(t)], bank4(bank), ACT.Exp))
        diff = step(dve, [rows, work_free, grown], lambda q: q.tensor_tensor(d, four(p.m("causal_neg")), bank4(bank), ALU.subtract))
        p.bank.give(bi, grown, diff)
        act.after(diff)
        for h in heads:
            decay_ready[t] = act.mark(act.q.activation(
                d[:, h, :], d[:, h, :], ACT.Exp, bias=s.cum[:, t, g * CT + h:g * CT + h + 1]))
        yield

    for k_ready in l2_normalise(p, kt, s.conv_ready[g, 1], 1.0, 0):
        yield

    a_t_ready, qk_ready, scaled = [None] * TT, [None] * TT, [None] * TT
    for t in range(TT):
        a, at, d = s.a[t], s.a_t[t], s.decay[t]
        bi, bank, bfree = p.bank.take()
        pe.after(k_ready, bfree)
        for h in heads:
            ins = pe.q.matmul(bank[:, row(h)], kt[:, h, row(t)], kt[:, h, row(t)], start=True, stop=True)
        kk = pe.mark(ins)
        dve.after(kk, decay_ready[t], work_free)
        for h in heads:
            made = dve.mark(dve.q.scalar_tensor_tensor(
                out=a[:, h, :], in0=bank[:, row(h)], scalar=s.beta[:, t, g * CT + h:g * CT + h + 1],
                in1=d[:, h, :], op0=ALU.mult, op1=ALU.mult))
        p.bank.give(bi, made)
        s.a_ready[t] = made
        bi, bank, bfree = p.bank.take()
        pe.after(q_ready, bfree)
        for h in heads:
            ins = pe.q.matmul(bank[:, row(h)], qt[:, h, row(t)], kt[:, h, row(t)], start=True, stop=True)
        qk = pe.mark(ins)
        scaled[t] = step(dve, [qk, work_free], lambda q: q.tensor_tensor(s.qk_t[t], bank4(bank), d, ALU.mult))
        p.bank.give(bi, scaled[t])
        yield
    for t in range(TT):
        a, at = s.a[t], s.a_t[t]
        bi, bank, bfree = p.bank.take()
        pe.after(s.a_ready[t], bfree)
        turned = transposes(p, bank, [a[:, h, :] for h in heads])
        a_t_ready[t] = step(act, [turned, work_free], lambda q: q.activation(at, bank4(bank), ACT.Copy))
        p.bank.give(bi, a_t_ready[t])
        bi, bank, bfree = p.bank.take()
        pe.after(scaled[t], bfree)
        turned = transposes(p, bank, [s.qk_t[t][:, h, :] for h in heads])
        qk_ready[t] = step(act, [turned], lambda q: q.activation(s.qk_t[t], bank4(bank), ACT.Copy))
        p.bank.give(bi, qk_ready[t])
        yield
    grown_q = step(dve, [qk, grown], lambda q: q.tensor_tensor(qt, qt, eg, ALU.mult))
    ends = eg.rearrange("p h (c i) -> p h c i", i=CHUNK)[:, :, :, CHUNK - 1]
    last_ready = step(dve, [grown, work_free], lambda q: q.tensor_copy(s.last, ends))
    p.scratch.give(eg_i, grown_q, last_ready)

    inv_ready, u_ready = [None] * TT, [None] * TT
    for t in range(TT):
        a, at, u = s.a[t], s.a_t[t], s.u[t]
        for src, mask, out, ready in ((at, "merge1_t", u, u_ready), (a, "merge1", a, inv_ready)):
            m1 = step(dve, [a_t_ready[t], s.a_ready[t], work_free],
                      lambda q: q.tensor_tensor(out, src, four(p.m(mask)), ALU.mult))
            ready[t] = step(dve, [m1], lambda q: q.scalar_tensor_tensor(
                out=out, in0=out, scalar=-1.0, in1=four(p.m("identity")), op0=ALU.mult, op1=ALU.add))
    yield
    y_read = [decay_ready[t] for t in range(TT)]
    for n in range(2, 7):
        y_done, off_i = [None] * TT, [None] * TT
        for t in range(TT):
            at, inv, y = s.a_t[t], s.a[t], s.decay[t]
            i, off, free = p.scratch.take()
            masked = step(pool, [a_t_ready[t], free], lambda q: q.tensor_tensor(
                off[:, :, 0:P], at, four(p.m(f"merge{n}_t")), ALU.mult))
            bi, bank, bfree = p.bank.take()
            pe.after(masked, inv_ready[t], bfree)
            for h in heads:
                ins = pe.q.matmul(bank[:, row(h)], off[:, h, 0:P], inv[:, h, :], start=True, stop=True)
            made = pe.mark(ins)
            p.scratch.give(i, made)
            y_done[t] = step(act, [made, y_read[t], scaled[t]], lambda q: q.activation(y, bank4(bank), ACT.Copy))
            p.bank.give(bi, y_done[t])
        yield
        for t in range(TT):
            inv, u, y = s.a[t], s.u[t], s.decay[t]
            if n < 6:
                bi, bank, bfree = p.bank.take()
                pe.after(y_done[t], u_ready[t], bfree)
                for h in heads:
                    ins = pe.q.matmul(bank[:, row(h)], u[:, h, :], y[:, h, :], start=True, stop=True)
                made = pe.mark(ins)
                inv_ready[t] = step(dve, [made], lambda q: q.tensor_tensor(inv, inv, bank4(bank), ALU.subtract))
                p.bank.give(bi, inv_ready[t])
            bi, bank, bfree = p.bank.take()
            pe.after(y_done[t], u_ready[t], bfree)
            for h in heads:
                ins = pe.q.matmul(bank[:, row(h)], y[:, h, :], u[:, h, :], start=True, stop=True)
            y_read[t] = made = pe.mark(ins)
            u_ready[t] = step(dve, [made], lambda q: q.tensor_tensor(u, u, bank4(bank), ALU.subtract))
            p.bank.give(bi, u_ready[t])
        yield

    kb_i, kb, kb_free = p.scratch.take()
    kb = kb.rearrange("p k t -> p (k t)").rearrange("p (t h n) -> p t h n", t=TT, h=CT)
    kb_ready, kd_ready = [None] * TT, [None] * TT
    for t in range(TT):
        bi, bank, bfree = p.bank.take()
        pe.after(k_ready, bfree)
        turned = transposes(p, bank, [kt[:, h, row(t)] for h in heads])
        act.after(turned, kb_free)
        for h in heads:
            c = g * CT + h
            kb_ready[t] = act.mark(act.q.activation(
                kb[:, t, h, :], bank[:, row(h)], ACT.Copy, scale=s.beta_decay[:, t, c:c + 1]))
        dve.after(kb_ready[t], y_read[t])
        for h in heads:
            c = g * CT + h
            kd_ready[t] = dve.mark(dve.q.tensor_scalar(
                s.decay[t][:, h, :], bank[:, row(h)], s.k_decay[:, t, c:c + 1], None, ALU.mult))
        p.bank.give(bi, kb_ready[t], kd_ready[t])
        yield

    while s.v_ready[g] is None:
        yield
    v_ready, w_ready = [None] * TT, [None] * TT
    for t in range(TT):
        u, w, v = s.u[t], s.a_t[t], s.a[t]
        bi, bank, bfree = p.bank.take()
        pe.after(u_ready[t], s.v_ready[g], bfree)
        for h in heads:
            ins = pe.q.matmul(bank[:, row(h)], u[:, h, :], vb[:, t, h, :], start=True, stop=True)
        made = pe.mark(ins)
        v_ready[t] = step(act, [made], lambda q: q.activation(v, bank4(bank), ACT.Copy))
        p.bank.give(bi, v_ready[t])
        bi, bank, bfree = p.bank.take()
        pe.after(kb_ready[t], bfree)
        for h in heads:
            ins = pe.q.matmul(bank[:, row(h)], kb[:, t, h, :], u[:, h, :], start=True, stop=True)
        made = pe.mark(ins)
        w_ready[t] = step(act, [made], lambda q: q.activation(w, bank4(bank), ACT.Copy))
        p.bank.give(bi, w_ready[t])
    p.scratch.give(kb_i, made)
    yield

    o, state = s.o[g], s.state
    state_ready = o_ready = None
    for c in range(T // CHUNK):
        t, half = divmod(c, TT)
        r = slice(half * CHUNK, (half + 1) * CHUNK)
        tok = slice(c * CHUNK, (c + 1) * CHUNK)
        v, w, kd, qk = s.a[t], s.a_t[t], s.decay[t], s.qk_t[t]
        if c > 0:
            bi, bank, bfree = p.bank.take()
            pe.after(state_ready, w_ready[t], bfree)
            for h in heads:
                ins = pe.q.matmul(bank[r, row(h)], w[:, h, r], state[:, h, :], start=True, stop=True)
            made = pe.mark(ins)
            new = step(dve, [made, v_ready[t]], lambda q: q.tensor_tensor(v[r], v[r], bank4(bank)[r], ALU.subtract))
            p.bank.give(bi, new)
            yield
        else:
            new = v_ready[t]
        if c < T // CHUNK - 1:
            bi, bank, bfree = p.bank.take()
            pe.after(new, kd_ready[t], bfree)
            for h in heads:
                ins = pe.q.matmul(bank[:, row(h)], kd[r, h, :], v[r, h, :], start=True, stop=True)
            made = pe.mark(ins)
            grown_bank, grown_i = bank, bi
        oi, obank, ofree = p.bank.take()
        pe.after(grown_q, qk_ready[t], new, ofree)
        for h in heads:
            out = obank[:, h * CHUNK:(h + 1) * CHUNK]
            if c > 0:
                pe.q.matmul(out, state[:, h, :], qt[:, h, tok], start=True, stop=False)
            ins = pe.q.matmul(out, v[r, h, :], qk[r, h, r], start=c == 0, stop=True)
        o_made = pe.mark(ins)
        if c < T // CHUNK - 1:
            if c == 0:
                state_ready = step(dve, [made, work_free], lambda q: q.tensor_copy(state, bank4(grown_bank)))
            else:
                dve.after(o_made)
                for h in heads:
                    state_ready = dve.mark(dve.q.scalar_tensor_tensor(
                        out=state[:, h, :], in0=state[:, h, :], scalar=s.last[:, h, c:c + 1],
                        in1=grown_bank[:, row(h)], op0=ALU.mult, op1=ALU.add))
            p.bank.give(grown_i, state_ready)
        o_ready = step(act, [o_made], lambda q: q.activation(
            o[:, :, tok], obank[:, 0:CT * CHUNK].rearrange("p (h n) -> p h n", h=CT), ACT.Copy))
        p.bank.give(oi, o_ready)
        yield
    s.chunks_done[g] = o_made

    while s.z_ready[g] is None:
        yield
    for s.o_ready[g] in head_norm(p, o, o_ready, "gdn_norm_g_2", z, s.z_ready[g]):
        yield


def attention_head(p, q_t, k_t, v, ready, out, out_free, scale, tiles, bias, small, state):
    pe, dve, act = p.pe, p.dve, p.act
    width = [n * P for n in tiles]
    at = [0, width[0]]
    total = sum(width)
    neg_max, total_p, inv = small[:, 0, :], small[:, 1, :], small[:, 2, :]
    i, buf, free = p.scratch.take()
    flat = buf.rearrange("p k t -> p (k t)")
    e, p_t = flat[:, 0:512], flat[:, 512:1024]
    bi, bank, bfree = p.bank.take()
    pe.after(ready, bfree)
    for t in range(TT):
        ins = pe.q.matmul(bank[:, at[t]:at[t] + width[t]], q_t[:, t * P:(t + 1) * P], k_t[:, 0:width[t]], start=True, stop=True)
    scores = pe.mark(ins)
    yield
    if bias is not None:
        added = bias(bank, e, [scores, free], scale, at, width)
        p.bank.give(bi, added)
        src, scale_in, src_ready = e, 1.0, added
    else:
        src, scale_in, src_ready = bank, scale, scores
    dve.after(src_ready)
    for t in range(TT):
        m1 = dve.mark(dve.q.tensor_reduce(neg_max[:, t:t + 1], src[:, at[t]:at[t] + width[t]], AX.X, ALU.max))
    m1 = step(dve, [m1], lambda q: q.tensor_scalar(neg_max, neg_max, -scale_in, None, ALU.mult))
    yield
    act.after(m1, free)
    for t in range(TT):
        seg = slice(at[t], at[t] + width[t])
        ex = act.mark(act.q.activation(e[:, seg], src[:, seg], ACT.Exp, bias=neg_max[:, t:t + 1],
                                                          scale=scale_in, accum_out=total_p[:, t:t + 1]))
    if bias is None:
        p.bank.give(bi, ex)
    m2 = step(dve, [ex], lambda q: q.reciprocal(inv, total_p))
    dve.after(m2)
    for t in range(TT):
        seg = slice(at[t], at[t] + width[t])
        m3 = dve.mark(dve.q.tensor_scalar(e[:, seg], e[:, seg], inv[:, t:t + 1], None, ALU.mult))
    yield
    blocks = [(t, k) for k in range(max(tiles)) for t in range(TT) if k < tiles[t]]
    bi, bank, bfree = p.bank.take()
    pe.after(m3, bfree)
    turned = transposes(p, bank, [e[:, at[t] + k * P:at[t] + (k + 1) * P] for t, k in blocks])
    c = step(act, [turned], lambda q: q.activation(p_t[:, 0:total], bank[:, 0:total], ACT.Copy))
    p.bank.give(bi, c)
    yield
    bi, bank, bfree = p.bank.take()
    pe.after(c, bfree)
    for k in range(max(tiles)):
        mine = [n for n, (t, kk) in enumerate(blocks) if kk == k]
        first_t = blocks[mine[0]][0]
        ins = pe.q.matmul(bank[:, first_t * P:T], v[k], p_t[:, mine[0] * P:(mine[-1] + 1) * P],
                          start=k == 0, stop=k == max(tiles) - 1, skip_group_check=True)
    made = pe.mark(ins)
    p.scratch.give(i, made)
    done = step(act, [made, out_free], lambda q: q.activation(out, bank[:, 0:T], ACT.Copy))
    p.bank.give(bi, done)
    state.append(done)
    yield


def pipeline(generators, depth):
    waiting, live = list(generators), []
    while waiting or live:
        if waiting and len(live) < depth:
            live.append(waiting.pop(0))
        live = [x for x in live if next(x, "end") != "end"]
        yield


class MixerMemory:
    pass


def token_column(p, s):
    i, bank, free = p.bank.take()
    p.pe.after(p.done["mix_norm", "row"], free)
    for t in range(TT):
        ins = p.pe.q.transpose(bank[:, t * P:(t + 1) * P], p.row["mix_norm"][:, t * P:(t + 1) * P], p.m("identity"))
    turned = p.pe.mark(ins)
    columns = bank[:, 0:T].rearrange("p (t n) -> p t n", t=TT)[:, :, 0]
    s.token_ready = step(p.act, [turned], lambda q: q.activation(s.token_col, columns, ACT.Copy))
    p.bank.give(i, s.token_ready)


def mixer(p, outer):
    d, dve, act, pe, stack = p.dram, p.dve, p.act, p.pe, ExitStack()
    s = MixerMemory()
    inputs = [p.sbuf(f"heads{g}", [P, 4, CT, T], stack=outer) for g in range(2)]
    p.inputs = inputs
    sb = lambda name, shape, dt=F32: p.sbuf(name, shape, dt, stack)
    s.w_ba_hi, s.w_ba_lo = sb("w_ba_hi", [P, KT, 16], F32R), sb("w_ba_lo", [P, KT, 16], F32R)
    s.dt_bias, s.a_log = sb("dt_bias", [P, NG]), sb("a_log", [P, NG])
    s.beta, s.g, s.cum, s.k_decay, s.beta_decay = (sb(n, [P, TT, NG]) for n in ("beta", "log_decay", "cum", "k_decay", "beta_decay"))
    s.small, s.ba, s.token_col = sb("gate_small", [P, 3, TT, NG]), sb("ba", [P, TT, 2 * NG]), sb("token_column", [P, TT])
    s.q_t, s.k_t, s.z = ([x[:, n] for x in inputs] for n in range(3))
    s.v_beta = [x[:, 3].rearrange("p k t -> p (k t)").rearrange("p (t h n) -> p t h n", t=TT, h=CT) for x in inputs]
    s.o = [sb(f"delta_out{g}", [P, CT, T]) for g in range(2)]
    s.w_ba = s.o[1].rearrange("p k t -> p (k t)")[:, 0:KT * 2 * NG].rearrange("p (k n) -> p k n", k=KT)
    work = sb("delta_work", [P, 5, TT, CT, P])
    s.decay, s.a, s.a_t, s.u, s.qk_t = ([work[:, n, t] for t in range(TT)] for n in range(5))
    s.state, s.last = sb("state", [P, CT, HD]), sb("last_decay", [P, CT, T // CHUNK])
    s.pad = Ring([sb("conv_pad", [P, CT, GDN_K - 1 + T])])
    v_own = sb("moba_v", [P, TT, NM * HD])
    small = s.qk_t[0].rearrange("p h n -> p (h n)")[:, 0:NM * 3 * TT].rearrange("p (h a t) -> p h a t", h=NM, a=3)
    s.conv_ready, s.a_ready, s.chunks_done, s.gates_ready = {}, [None] * TT, [None] * 2, None
    s.v_ready, s.z_ready, s.o_ready, s.delta_done = [None] * 2, [None] * 2, [None] * 2, [False] * 2

    def start():
        p.phase()
        load_gates()
        two_norms(p)

    def load_gates():
        gate_columns = d["w_in_2"][:, 4 * GW:4 * GW + 2 * NG]
        s.w_ba_landed = p.dma(act, s.w_ba, gate_columns.rearrange("(k p) n -> p k n", p=P), "w_ba_landed")
        p.dma(act, s.dt_bias, d["dt_bias"].partition_broadcast(P), "heads_landed")
        s.heads_landed = p.dma(act, s.a_log, d["a_log"].partition_broadcast(P), "heads_landed")
        s.pad.give(0, step(p.pool, [], lambda q: q.memset(s.pad.buffers[0][:, :, 0:GDN_K - 1], 0.0)))

    def v_block(g):
        def evict(psum, mark):
            i, v, free = p.scratch.take()
            copied = conv_silu(p, s, g, 2, v, free)(psum, mark)
            s.pending.append([TURN_AFTER, g, i, v])
            return copied
        return evict

    def turn_v(g, i, v):
        for t in range(TT):
            bi, bank, bfree = p.bank.take()
            pe.after(s.conv_ready[g, 2], bfree)
            turned = transposes(p, bank, [v[:, h, t * P:(t + 1) * P] for h in range(CT)])
            act.after(turned, s.gates_ready)
            for h in range(CT):
                c = g * CT + h
                done = act.mark(act.q.activation(
                    s.v_beta[g][:, t, h, :], bank[:, h * P:(h + 1) * P], ACT.Copy, scale=s.beta[:, t, c:c + 1]))
            p.bank.give(bi, done)
        p.scratch.give(i, turned)
        s.v_ready[g] = done

    def z_block(g):
        def evict(psum, mark):
            scaled = p.times_row("mix_norm", s.z[g], psum, [mark])
            s.z_ready[g] = step(act, [scaled], lambda q: q.activation(s.z[g], s.z[g], ACT.Silu))
            return scaled
        return evict

    def copy_out(dst, key):
        def evict(psum, mark):
            assert s.delta_done[0]
            moba_ready[key] = p.times_row("mix_norm", dst, psum, [mark, s.chunks_done[0], s.o_ready[0]])
            return moba_ready[key]
        return evict

    def copy_tokens(dst, key):
        def evict(psum, mark):
            act.after(mark, s.token_ready)
            for t in range(TT):
                moba_ready[key] = act.mark(act.q.activation(
                    dst[:, t, :], psum[:, t * COLS:(t + 1) * COLS], ACT.Copy, scale=s.token_col[:, t:t + 1]))
            return moba_ready[key]
        return evict

    s.pending = []
    moba_ready = {}
    mq = inputs[0][:, 0:2].rearrange("p a k t -> p (a k) t")
    mk = inputs[0][:, 2:4].rearrange("p a k t -> p (a k) t")

    def products():
        for g in range(2):
            q = p.product("w_in_2", g * COLS, p.h, "mix_norm", conv_silu(p, s, g, 0, s.q_t[g], None))
            yield from with_row(q, start) if g == 0 else q
            k = p.product("w_in_2", GW + g * COLS, p.h, "mix_norm", conv_silu(p, s, g, 1, s.k_t[g], None))
            beside = gates(p, s) if g == 0 else iter(())
            v = p.product("w_in_2", 2 * GW + g * COLS, p.h, "mix_norm", v_block(g))
            for product in (k, v):
                for _ in product:
                    next(beside, None)
                    yield
            yield from p.product("w_in_2", 3 * GW + g * COLS, p.h, "mix_norm", z_block(g))
        base = 4 * GW + 2 * NG
        for b in MOBA_BLOCKS:
            if b < 4:
                dst = (mq, mk)[b // 2][:, (b % 2) * CT:(b % 2 + 1) * CT, :]
                yield from p.product("w_in_2", base + b * COLS, p.h, "mix_norm", copy_out(dst, b))
            else:
                half = v_own[:, :, (b - 4) * COLS:(b - 3) * COLS]
                yield from p.product("w_in_2", base + b * COLS, p.h, "mix_norm", copy_tokens(half, b), tokens_out=True)

    bias_sb = work[:, 0:2].rearrange("p a t h n -> p (a t h n)").rearrange("p (h j) -> p h j", h=NM)
    o_b = inputs[1][:, 0:2].rearrange("p a k t -> p (a k) t")
    heads_done = []

    def moba_bias(h):
        def add(bank, e, marks, scale, at, width):
            m1 = step(dve, [marks, s.bias_landed], lambda q: q.scalar_tensor_tensor(
                out=e[:, 0:P], in0=bank[:, 0:P], scalar=scale, in1=bias_sb[:, h, P:T], op0=ALU.mult, op1=ALU.add))
            return step(dve, [marks, m1], lambda q: q.scalar_tensor_tensor(
                out=e[:, P:P + T], in0=bank[:, P:P + T], scalar=scale, in1=bias_sb[:, h, :], op0=ALU.mult, op1=ALU.add))
        return add

    def one(h):
        cols = slice(h * HD, (h + 1) * HD)
        blocks = [h // CT, 2 + h // CT, 4 + h // CT]
        while not all(b in moba_ready for b in blocks):
            yield
        ready = [moba_ready[b] for b in blocks]
        yield from attention_head(p, mq[:, h, :], mk[:, h, :], [v_own[:, 0, cols], v_own[:, 1, cols]], ready,
                              o_b[:, h, :], [s.chunks_done[1], s.o_ready[1]], HD ** -0.5, [1, 2], moba_bias(h), small[:, h], heads_done)

    def load_bias():
        p.sp.after(s.chunks_done[1], p.bias_rows_stored)
        skew = bass.AP(d["bias_rows"].tensor, P - 1, [[BIAS_W - 1, P], [P * BIAS_W, NM], [1, T]])
        s.bias_landed = p.dma(p.sp, bias_sb, skew, "bias_landed")

    def sides():
        for g in range(2):
            while (g, 1) not in s.conv_ready or s.gates_ready is None:
                yield
            yield from delta_rule(p, s, g)
            s.delta_done[g] = True
        load_bias()
        yield from pipeline([one(h) for h in range(NM)], 3)
        while not w_in_done:
            yield
        for g in range(2):
            ob = o_b[:, g * CT:(g + 1) * CT, :]
            for done in head_norm(p, ob, heads_done[g * CT:(g + 1) * CT], "moba_norm_g_2"):
                yield
            p.moba_split = p.split_into(ob, done, p.h, (2 + g) * CT, CT, "heads_out", p.done["w_in_2"])

    w_in_done = []
    side = sides()
    for _ in products():
        if s.pending:
            s.pending[0][0] -= 1
            if s.pending[0][0] == 0:
                turn_v(*s.pending.pop(0)[1:])
        next(side, None)
    w_in_done.append(True)
    for g in range(2):
        while s.o_ready[g] is None or not s.delta_done[g]:
            next(side)
        p.split_into(s.o[g], s.o_ready[g], p.h, g * CT, CT, "heads_out", p.done["w_in_2"])

    parts = [{} for _ in range(CT)]
    after = [None]

    def out_evict(b):
        return lambda psum, mark: p.residual("mixer", b, [("final1", "group", b)], after=after[0])(psum, mark)

    def w_out(order):
        for half, b in order:
            yield from p.product("w_out_2", b * COLS, p.h, "heads_out", out_evict(b), row=half * GW,
                                 k_tiles=range(half * KT // 2, (half + 1) * KT // 2), part_of=(parts[b], half == 0, half == 1))
    for _ in w_out(w_out_order()[:2]):
        for _ in range(OUT_STEPS):
            next(side, None)
    run(side)
    stack.close()
    p.phase()
    p.mid = Operand(p.sbuf("mid2_hi", [P, KT, T], F32R, outer), p.sbuf("mid2_lo", [P, KT, T], F32R, outer))
    after[0] = p.next_operand("xattn_norm", p.gain("xattn_norm_g_2"), p.mid, None)
    run(w_out(w_out_order()[2:]))



def cross_attention(p, outer):
    q_t, o = p.inputs[0][:, 0], p.inputs[0][:, 1]
    small = p.sbuf("cross_small", [P, NX, 3, TT], stack=outer)
    x_o = Operand(p.h.hi[:, 0:NX, :], p.h.lo[:, 0:NX, :])
    ready = []

    def evict(psum, mark):
        ready.append(p.times_row("xattn_norm", q_t, psum, [mark, p.moba_split]))
        return ready[-1]
    run(with_row(p.product("w_xq_2", 0, p.mid, "xattn_norm", evict),
                 lambda: p.rms_row("xattn_norm", p.done["final1", "applied"])))
    done = []

    def one(h):
        cols = slice(h * HD, (h + 1) * HD)
        return attention_head(p, q_t[:, h, :], p.mem_k[:, h, :], [p.mem_v[:, 0, cols], p.mem_v[:, 1, cols]],
                              [ready, p.mem_k_ready, p.mem_v_ready], o[:, h, :], p.moba_split, HD ** -0.5, [2, 2],
                              None, small[:, h], done)
    run(pipeline([one(h) for h in range(NX)], 3))
    p.cross_split = p.split_into(o, done, x_o, 0, NX, "cross_out", p.done["w_out_2"])
    after = p.next_operand("ffn_norm", p.gain("ffn_norm_g_2"), p.mid, "w_xq_2")
    for b in range(CT):
        before = [("mixer", b), ("xattn_norm", "scaled", b), ("xattn_norm", "squares", b)]
        run(p.product("w_xo_2", b * COLS, x_o, "cross_out", p.residual("cross", b, before, after=after)))


def conv_ffn(p):
    dve, act = p.dve, p.act
    spare = p.inputs[1].rearrange("p a k t -> p (a k t)")
    wide = FFN_K - 1 + T
    pads = Ring([spare[:, i * CT * wide:(i + 1) * CT * wide].rearrange("p (k t) -> p k t", k=CT) for i in range(2)])
    gate = Ring([p.inputs[0][:, 2 + i] for i in range(2)])
    for i in range(2):
        pads.give(i, step(p.pool, [p.moba_split], lambda q: q.memset(pads.buffers[i][:, :, 0:FFN_K - 1], 0.0)))
    mids = [Operand(p.h.hi[:, i * CT:(i + 1) * CT, :], p.h.lo[:, i * CT:(i + 1) * CT, :]) for i in range(3)]
    gates_ready = {}

    def evict_gate(c):
        def evict(psum, mark):
            i, pad, free = pads.take()
            copied = p.times_row("ffn_norm", pad[:, :, FFN_K - 1:], psum, [mark, free])
            gi, g, gfree = gate.take()
            done = [None] * CT

            def taps(j):
                if j == 0:
                    dve.after(copied, gfree)
                for t in range(CT):
                    w = p.col("ffn_conv_w_2", (c * CT + t) * FFN_K + j)
                    tap = pad[:, t, j:j + T]
                    if j == 0:
                        b = p.col("ffn_conv_b_2", c * CT + t)
                        done[t] = dve.mark(dve.q.tensor_scalar(g[:, t, :], tap, w, b, ALU.mult, ALU.add))
                    else:
                        done[t] = step(dve, [done[t]], lambda q: q.scalar_tensor_tensor(
                            out=g[:, t, :], in0=tap, scalar=w, in1=g[:, t, :], op0=ALU.mult, op1=ALU.add))
                if j == FFN_K - 1:
                    pads.give(i, done[-1])

            def gated():
                silu = step(act, [done[-1]], lambda q: q.activation(g, g, ACT.Silu))
                scaled = step(p.pool, [silu, p.done["ffn_norm", "row"]], lambda q: q.tensor_tensor(
                    g, g, p.row["ffn_norm"].unsqueeze(1).broadcast_to([P, CT, T]), ALU.mult))
                gates_ready[c] = (gi, g, scaled)
            for j in range(FFN_K):
                p.put_off(lambda j=j: taps(j))
            p.put_off(gated, 2)
            return copied
        return evict

    def evict_up(c, mid):
        def evict(psum, mark):
            gi, g, g_done = gates_ready[c]
            made = step(dve, [mark, g_done], lambda q: q.tensor_tensor(g, g, psum.rearrange("p (k t) -> p k t", t=T), ALU.mult))
            used = p.done["w_down_2"] if c >= 3 else p.done["w_xo_2"]
            gate.give(gi, p.split_into(g, made, mid, 0, CT, ("ffn_hidden", c), used))
            return made
        return evict

    last = DFF2 // COLS - 1
    after = p.next_operand("final2", None, None, None)
    for kind, c in ffn_order():
        mid = mids[c % 3]
        if kind == "up":
            up = p.product("w_gate_2", c * COLS, p.mid, "ffn_norm", evict_gate(c))
            if c == 0:
                up = with_row(up, lambda: p.rms_row("ffn_norm", p.done["mix_norm", "applied"]))
            run(up)
            run(p.product("w_up_2", c * COLS, p.mid, "ffn_norm", evict_up(c, mid)))
        else:
            for b in range(CT):
                before = [(("ffn", c - 1), b)] if c else [("cross", b), ("ffn_norm", "scaled", b), ("ffn_norm", "squares", b)]
                add = p.residual(("ffn", c), b, before, after=after if c == last else None)
                run(p.product("w_down_2", b * COLS, mid, ("ffn_hidden", c), add, row=c * COLS))


def build(nc, dram):
    with ExitStack() as stack:
        p = Program(nc, stack, dram)
        p.plan_weights()
        with ExitStack() as p.phase_stack:
            conformer(p)
            mlp(p)
        with ExitStack() as outer:
            p.pool_every = 2
            mixer(p, outer)
            p.pool_every = 0
            cross_attention(p, outer)
            conv_ffn(p)
            last_norm(p)
            store_x(p)



WEIGHTS = ["cc_w_in", "cc_w_out", "mlp_w1", "mlp_w2", "w_in_2", "w_out_2", "w_xq_2", "w_xkv_2", "w_xo_2",
           "w_gate_2", "w_up_2", "w_down_2"]


def layout(inputs):
    a = {}
    for name, key in (("x", "x"), ("mem", "mem_2")):
        a[name] = np.ascontiguousarray(np.asarray(inputs[key])[0].T.reshape(KT, P, T))
    for name in WEIGHTS:
        w = np.asarray(inputs[name])
        a[name] = np.ascontiguousarray(w[0])
    parts = []
    for name, tiles in VECTORS:
        parts.append(np.asarray(inputs[name]).reshape(tiles, P).T)
    for name, tiles, taps in FILTERS:
        parts.append(np.asarray(inputs[name]).reshape(taps, tiles, P).transpose(2, 1, 0).reshape(P, tiles * taps))
    a["feature_columns"] = np.ascontiguousarray(np.concatenate(parts, axis=1))
    a["masks"] = np.ascontiguousarray(masks())
    hot, neg = bucket_rows()
    a["bucket_one_hot"], a["bucket_neg"] = hot, neg
    a["rel_bias"] = np.ascontiguousarray(np.asarray(inputs["rel_bias_2"]))
    a["a_log"] = np.ascontiguousarray(np.asarray(inputs["gdn_a_log_2"]))
    a["dt_bias"] = np.ascontiguousarray(np.asarray(inputs["gdn_dt_bias_2"]))
    return a


def kernel(**inputs):
    import concourse.bacc as bacc
    from concourse.bass_utils import run_bass_kernel_spmd

    nc = bacc.Bacc("TRN2", target_bir_lowering=False, num_devices=1)
    arrays, dram = {}, {}
    for name, a in layout(inputs).items():
        arrays[f"in_{name}"] = a
        dram[name] = nc.dram_tensor(f"in_{name}", a.shape, mybir.dt.from_np(a.dtype), kind="ExternalInput").ap()
    dram["out"] = nc.dram_tensor("out_features", [KT, P, T], F32, kind="ExternalOutput").ap()
    dram["bias_rows"] = nc.dram_tensor("bias_rows", [NM, P, BIAS_W], F32, kind="Internal").ap()
    build(nc, dram)
    r = run_bass_kernel_spmd(nc, [arrays], core_ids=[0])
    return np.ascontiguousarray(r.results[0]["out_features"].reshape(D, T).T)[None]
```
